# Optimizing a Trainium2 kernel written in Bass

```python
import jax, jax.numpy as jnp
from jax import lax
import numpy as np

D_MODEL = 2048
BATCH = 1
SEQ = 256
DEPTH = 1
DEC_BATCH = 8
DEC_SEQ = 4
PAST_LEN = 256
PAGE_SIZE = 128

N_HEADS = 16
HEAD_DIM = 64
D_ATTN = N_HEADS * HEAD_DIM
D_CONV = 1024
CONV_W = 3
D_FF = ((8 * D_MODEL // 3 + 255) // 256) * 256
Q_BLOCK = 128
RMS_EPS = 1e-6
ATTN_SCALE = HEAD_DIM ** -0.5
FORGET_BIAS_INIT = 4.0
IN_SIZES = (D_ATTN, D_ATTN, D_ATTN, N_HEADS, D_CONV, D_CONV, D_CONV, D_MODEL, D_MODEL)
N_IN = sum(IN_SIZES)

kernel_name = "fox_shortconv_gated_hybrid_step"

def _rmsnorm(x, g):
    xf = x.astype(jnp.float32)
    y = xf * lax.rsqrt(jnp.mean(xf * xf, axis=-1, keepdims=True) + RMS_EPS)
    return (y * g.astype(jnp.float32)).astype(x.dtype)

def _split_cols(z, sizes):
    offs = np.cumsum(sizes)[:-1].tolist()
    return jnp.split(z, offs, axis=-1)

def _adaln(c, w_ada, b_ada):
    m = jax.nn.silu(c) @ w_ada + b_ada
    return jnp.split(m[:, None, :], 6, axis=-1)

def _mixer_inputs(x, shift, scale, g_pre, w_in, b_f):
    B, T, _ = x.shape
    h = _rmsnorm(x, g_pre) * (1.0 + scale) + shift
    q, k, v, f, u, bg, cg, ga, gb = _split_cols(h @ w_in, IN_SIZES)
    logf = jax.nn.log_sigmoid((f + b_f).astype(jnp.float32))
    heads = lambda t: t.reshape(B, T, N_HEADS, HEAD_DIM)
    return heads(q), heads(k), heads(v), logf, cg * u, bg, ga, gb

def _fox_softmax(s, cum_q, cum_k, mask):
    bias = jnp.swapaxes(cum_q, 1, 2)[..., :, None] - jnp.swapaxes(cum_k, 1, 2)[..., None, :]
    logits = s.astype(jnp.float32) * ATTN_SCALE + bias.astype(jnp.float32)
    logits = jnp.where(mask, logits, -jnp.inf)
    return jax.nn.softmax(logits, axis=-1)

def _prompt_attention(q, k, v, cum):
    B, T, H, Dh = q.shape
    nb = T // Q_BLOCK
    qb = q.reshape(B, nb, Q_BLOCK, H, Dh).swapaxes(0, 1)
    cb = cum.reshape(B, nb, Q_BLOCK, H).swapaxes(0, 1)
    kpos = jnp.arange(T, dtype=jnp.int32)
    pb = kpos.reshape(nb, Q_BLOCK)

    def block(args):
        q_i, c_i, p_i = args
        s = jnp.einsum('bqhd,bkhd->bhqk', q_i, k)
        p = _fox_softmax(s, c_i, cum, kpos[None, :] <= p_i[:, None])
        return jnp.einsum('bhqk,bkhd->bqhd', p.astype(v.dtype), v)

    o = lax.map(block, (qb, cb, pb))
    return o.swapaxes(0, 1).reshape(B, T, H, Dh)

def _sample_attention(q, k_new, v_new, cum_q, cum_all, k_past, v_past):
    P = k_past.shape[1]
    T = q.shape[1]
    s = jnp.concatenate([jnp.einsum('bqhd,bkhd->bhqk', q, k_past),
                         jnp.einsum('bqhd,bkhd->bhqk', q, k_new)], axis=-1)
    qpos = P + jnp.arange(T, dtype=jnp.int32)
    kpos = jnp.arange(P + T, dtype=jnp.int32)
    p = _fox_softmax(s, cum_q, cum_all, kpos[None, :] <= qpos[:, None]).astype(v_new.dtype)
    return (jnp.einsum('bhqk,bkhd->bqhd', p[..., :P], v_past)
            + jnp.einsum('bhqk,bkhd->bqhd', p[..., P:], v_new))

def _conv_causal(zp, w_conv, T):
    y = zp[:, 0:T] * w_conv[0]
    for j in range(1, CONV_W):
        y = y + zp[:, j:j + T] * w_conv[j]
    return y

def _finish(x, o, y_conv, bg, ga, gb, gate1, shift2, scale2, gate2,
            w_oa, w_ob, w_o, g_post1, g_pre2, w_ffn_in, w_ffn_out, g_post2):
    B, T, _ = x.shape
    a = o.reshape(B, T, D_ATTN) @ w_oa
    b = (bg * y_conv) @ w_ob
    m = (jax.nn.sigmoid(ga) * a + jax.nn.sigmoid(gb) * b) @ w_o
    x = x + gate1 * _rmsnorm(m, g_post1)
    h = _rmsnorm(x, g_pre2) * (1.0 + scale2) + shift2
    g, u = jnp.split(h @ w_ffn_in, 2, axis=-1)
    f = (jax.nn.silu(g) * u) @ w_ffn_out
    return x + gate2 * _rmsnorm(f, g_post2)

def setup_inputs(seed: int = 0) -> dict:
    key = jax.random.key(seed)
    ks = jax.random.split(key, 24)
    n_pages = PAST_LEN // PAGE_SIZE
    n_pool = (DEC_BATCH * n_pages * 5) // 4
    nrm = lambda k, shape, s=1.0: jax.random.normal(k, shape, jnp.float32) * s
    page_table = jax.random.permutation(ks[0], n_pool)[:DEC_BATCH * n_pages]
    page_table = page_table.reshape(DEC_BATCH, n_pages).astype(jnp.int32)
    return {
        "x_prompt": nrm(ks[1], (BATCH, SEQ, D_MODEL)),
        "x_sample": nrm(ks[2], (DEC_BATCH, DEC_SEQ, D_MODEL)),
        "cache_k": nrm(ks[3], (DEPTH, n_pool, PAGE_SIZE, N_HEADS, HEAD_DIM)),
        "cache_v": nrm(ks[4], (DEPTH, n_pool, PAGE_SIZE, N_HEADS, HEAD_DIM)),
        "cache_logf": jax.nn.log_sigmoid(FORGET_BIAS_INIT + nrm(ks[5], (DEPTH, n_pool, PAGE_SIZE, N_HEADS), 0.5)),
        "state_conv": nrm(ks[6], (DEPTH, DEC_BATCH, CONV_W - 1, D_CONV)),
        "page_table": page_table,
        "c_prompt": nrm(ks[7], (BATCH, D_MODEL)),
        "c_sample": nrm(ks[8], (DEC_BATCH, D_MODEL)),
        "w_ada": nrm(ks[9], (DEPTH, D_MODEL, 6 * D_MODEL), 0.5 * D_MODEL ** -0.5),
        "b_ada": nrm(ks[10], (DEPTH, 6 * D_MODEL), 0.02),
        "g_pre1": 1.0 + nrm(ks[11], (DEPTH, D_MODEL), 0.02),
        "w_in": nrm(ks[12], (DEPTH, D_MODEL, N_IN), D_MODEL ** -0.5),
        "b_f": FORGET_BIAS_INIT + nrm(ks[13], (DEPTH, N_HEADS), 0.5),
        "w_conv": nrm(ks[14], (DEPTH, CONV_W, D_CONV), CONV_W ** -0.5),
        "w_oa": nrm(ks[15], (DEPTH, D_ATTN, D_MODEL), D_ATTN ** -0.5),
        "w_ob": nrm(ks[16], (DEPTH, D_CONV, D_MODEL), D_CONV ** -0.5),
        "w_o": nrm(ks[17], (DEPTH, D_MODEL, D_MODEL), D_MODEL ** -0.5),
        "g_post1": 1.0 + nrm(ks[18], (DEPTH, D_MODEL), 0.02),
        "g_pre2": 1.0 + nrm(ks[19], (DEPTH, D_MODEL), 0.02),
        "w_ffn_in": nrm(ks[20], (DEPTH, D_MODEL, 2 * D_FF), D_MODEL ** -0.5),
        "w_ffn_out": nrm(ks[21], (DEPTH, D_FF, D_MODEL), D_FF ** -0.5),
        "g_post2": 1.0 + nrm(ks[22], (DEPTH, D_MODEL), 0.02),
    }

def reference(x_prompt, x_sample, cache_k, cache_v, cache_logf, state_conv, page_table,
              c_prompt, c_sample, w_ada, b_ada, g_pre1, w_in, b_f, w_conv, w_oa, w_ob, w_o,
              g_post1, g_pre2, w_ffn_in, w_ffn_out, g_post2):
    n_pages = page_table.shape[1]
    xp, xs = x_prompt, x_sample
    kp_l, vp_l, fp_l, cp_l, ks_l, vs_l, fs_l, cs_l = [], [], [], [], [], [], [], []
    for l in range(DEPTH):
        shared = (w_oa[l], w_ob[l], w_o[l], g_post1[l], g_pre2[l], w_ffn_in[l], w_ffn_out[l], g_post2[l])
        sh1, sc1, gt1, sh2, sc2, gt2 = _adaln(c_prompt, w_ada[l], b_ada[l])
        q, k, v, logf, zc, bg, ga, gb = _mixer_inputs(xp, sh1, sc1, g_pre1[l], w_in[l], b_f[l])
        cum = jnp.cumsum(logf, axis=1)
        o = _prompt_attention(q, k, v, cum)
        T = xp.shape[1]
        y_conv = _conv_causal(jnp.pad(zc, ((0, 0), (CONV_W - 1, 0), (0, 0))), w_conv[l], T)
        xp = _finish(xp, o, y_conv, bg, ga, gb, gt1, sh2, sc2, gt2, *shared)
        kp_l.append(k); vp_l.append(v); fp_l.append(logf); cp_l.append(zc[:, T - (CONV_W - 1):])
        sh1, sc1, gt1, sh2, sc2, gt2 = _adaln(c_sample, w_ada[l], b_ada[l])
        q, k, v, logf, zc, bg, ga, gb = _mixer_inputs(xs, sh1, sc1, g_pre1[l], w_in[l], b_f[l])
        Bd, Ts = xs.shape[:2]
        k_past = cache_k[l][page_table].reshape(Bd, n_pages * PAGE_SIZE, N_HEADS, HEAD_DIM)
        v_past = cache_v[l][page_table].reshape(Bd, n_pages * PAGE_SIZE, N_HEADS, HEAD_DIM)
        f_past = cache_logf[l][page_table].reshape(Bd, n_pages * PAGE_SIZE, N_HEADS)
        P = n_pages * PAGE_SIZE
        cum_all = jnp.cumsum(jnp.concatenate([f_past.astype(jnp.float32), logf], axis=1), axis=1)
        o = _sample_attention(q, k, v, cum_all[:, P:], cum_all, k_past, v_past)
        zp = jnp.concatenate([state_conv[l].astype(zc.dtype), zc], axis=1)
        y_conv = _conv_causal(zp, w_conv[l], Ts)
        xs = _finish(xs, o, y_conv, bg, ga, gb, gt1, sh2, sc2, gt2, *shared)
        ks_l.append(k); vs_l.append(v); fs_l.append(logf); cs_l.append(zp[:, Ts:])
    return (xp, xs,
            jnp.stack(kp_l), jnp.stack(vp_l), jnp.stack(fp_l), jnp.stack(cp_l),
            jnp.stack(ks_l), jnp.stack(vs_l), jnp.stack(fs_l), jnp.stack(cs_l))


_drawn_inputs = setup_inputs


def setup_inputs(seed=0):
    import zlib

    import numpy as np

    out = dict(_drawn_inputs(seed))
    spreads = {}
    factors = {'cache_logf': 8.0, 'g_post1': 8.0, 'g_pre2': 23.221, 'g_post2': 33.091}
    for name, (base, spread) in spreads.items():
        noise = np.random.default_rng([zlib.crc32(name.encode()), seed]).standard_normal(out[name].shape)
        drawn = base * np.exp(spread * noise) if base else spread * noise
        out[name] = __import__('jax').numpy.asarray(drawn.astype(out[name].dtype))
    for name, factor in factors.items():
        out[name] = (out[name] * factor).astype(out[name].dtype)
    return out
```

```python
from contextlib import ExitStack, contextmanager

import numpy as np

import concourse.bass as bass
import concourse.mybir as mybir
from concourse.alu_op_type import AluOpType as ALU

F32 = mybir.dt.float32
F32R = mybir.dt.float32r
I32 = mybir.dt.int32
ACT = mybir.ActivationFunctionType
AX = mybir.AxisListType

P = 128
EPS = 1e-6
MASKED = -1e30
RAW = 4
SPLIT = 2
SK = 4
SN = 512
MT = SN // P


class Own:

    def __init__(self, eng, sem):
        self.eng, self.sem, self.n, self.turn = eng, sem, 0, 0

    def mark(self, ins):
        ins.then_inc(self.sem, 1)
        self.n += 1

    def step(self):
        self.eng.sem_inc(self.sem, 1)
        self.n += 1

    def wait(self):
        self.eng.wait_ge(self.sem, self.n + self.turn)

    @contextmanager
    def loop(self, count, per):
        start = self.n
        with self.eng.Fori(0, count) as i:
            self.turn = i * per
            yield i
            assert self.n - start == per, (self.n - start, per)
        self.turn = 0
        self.n = start + per * count


def layer(nc, x_prompt, x_sample, cache_k, cache_v, cache_logf, state_conv, page_table, c_prompt,
          c_sample, w_ada, b_ada, g_pre1, w_in, b_f, w_conv, w_oa, w_ob, w_o, g_post1, g_pre2,
          w_ffn_in, w_ffn_out, g_post2, y_prompt, y_sample, k_prompt, v_prompt, logf_prompt,
          conv_prompt, k_sample, v_sample, logf_sample, conv_sample):
    _, TP, D = x_prompt.shape
    SB, ST, _ = x_sample.shape
    TS = SB * ST
    NT = TP + TS
    _, POOL, PAGE, H, DH = cache_k.shape
    NPG = page_table.shape[1]
    DA = H * DH
    DC = w_conv.shape[2]
    CW = w_conv.shape[1]
    DFF = w_ffn_out.shape[1]
    KT = D // P
    KA = DA // P
    KC = DC // P
    KF = DFF // P
    NC = 1 + SB
    NMOD = 6
    SCALE = DH ** -0.5
    PAST = NPG * PAGE
    assert PAGE == P and NPG == 2 and DH == 64 and TP == 2 * P and CW == 3 and KT == 16
    assert KA == 8 and KC == 8 and NT + 0 <= 512 and KF == 11 * SK and SB == 8 and ST == 4
    CQ, CK, CV = 0, DA, 2 * DA
    CF = 3 * DA
    CU = CF + H
    CB, CC = CU + DC, CU + 2 * DC
    CGA = CU + 3 * DC
    CGB = CGA + D

    HALVES = DC // SN
    PER_HALF = 3 * KT // SK
    N_UCB = 0
    N_QKV = N_UCB + HALVES * PER_HALF
    N_MIX = N_QKV + HALVES * PER_HALF
    MIXES = D // SN
    PER_MIX = 2 * (KT // SK) + 2 * (KA // SK)
    N_O = N_MIX + MIXES * PER_MIX
    PER_O = KT // SK
    N_F1 = N_O + MIXES * PER_O
    F1S = DFF // SN
    PER_F1 = 2 * KT // SK
    N_F2 = N_F1 + F1S * PER_F1
    PER_F2 = 2 * (KF // SK)
    G_UCB = 0
    G_QKV = G_UCB + 3 * HALVES
    G_MIX = G_QKV + 3 * HALVES
    G_O = G_MIX + 4 * MIXES
    G_F1 = G_O + MIXES
    G_F2 = G_F1 + 2 * F1S
    G_END = G_F2 + MIXES
    BT = KT - MT
    R_PAGES = N_MIX // RAW
    PAGE_TURNS = SB // 2
    R_MIX = R_PAGES + NPG * PAGE_TURNS
    R_O = R_MIX + MIXES * PER_MIX // RAW
    R_F1 = R_O + MIXES * PER_O // RAW
    R_F2 = R_F1 + F1S * PER_F1 // RAW
    ADA_G = NMOD * D // SN
    ADA_FIRST = 2 * D // SN
    ADA_PER_HALF = (ADA_G - ADA_FIRST) // (2 * HALVES)
    assert ADA_PER_HALF == 4 and PER_HALF == 3 * ADA_PER_HALF

    ctx = ExitStack()
    with ctx:
        def sem(name):
            return ctx.enter_context(nc.semaphore(name))

        base = -(-nc.sbuf_base // 64) * 64
        at = [base]

        def place(name, shape, dt=F32, where=None):
            size = 4 * int(np.prod(shape[1:]))
            if where is None:
                where = at[0]
                at[0] += -(-size // 32) * 32
            assert where % 32 == 0, name
            return nc.alloc_sbuf_tensor_at(name, shape, dt, offset=where)

        ident = place("ident", [P, P])
        ones = place("ones", [P, TP])
        mask_q = place("mask_q", [P, TP])
        mask_s = place("mask_s", [P, SB * (TS + ST)])
        vecT = place("vecT", [P, 4 * KT + CW * KC])
        bT = place("bT", [P, NMOD * KT])
        mods = place("mods", [P, NMOD * KT, NC])
        modA = place("modA", [P, KT, NC])
        modG = place("modG", [P, KT, NC])
        o_cT = at[0]
        cT = place("cT", [P, KT, 32])
        lfc = place("lfc", [P, SB, NPG, H], where=o_cT)
        suf = place("suf", [P, SB, NPG, H], where=o_cT + SB * NPG * H * 4)
        sel = place("sel", [48, KA, 2 * ST])
        selq = place("selq", [48, KA, 32])
        cq = place("cq", [P, TS])
        lf = place("lf", [H, NT])
        lfr = place("lfr", [P, 3, H])
        bf = place("bf", [H, 1])
        small = place("small", [P, 16])
        table = place("table", [1, SB * NPG], I32)
        sqr = place("sqr", [P, NT], where=at[0])
        ada_sb = place("ada_sb", [P, SN])
        rstd = place("rstd", [P, NT])
        cum_q = place("cum_q", [P, TP], where=at[0] - -(-4 * NT // 32) * 32)

        off_raw = at[0]
        raw = [place(f"raw{s}", [P, SK, SN]) for s in range(RAW)]
        off_split = at[0]
        w_hi = [place(f"w_hi{s}", [P, SK, SN], F32R) for s in range(SPLIT)]
        w_lo = [place(f"w_lo{s}", [P, SK, SN], F32R) for s in range(SPLIT)]
        xT = place("xT", [P, KT, NT])
        off_act = at[0]
        a_hi = place("a_hi", [P, KT, NT], F32R)
        a_lo = place("a_lo", [P, KT, NT], F32R)
        R = at[0]
        top = nc.sbuf_usable_end
        assert R + 69632 + 4608 <= top, (R, top, top - R)
        B_ACT8 = KA * NT * 4
        ada = [place(f"ada{s}", [P, SK, SN], where=R + s * SK * SN * 4) for s in range(RAW)]
        o_qkv = R + RAW * SK * SN * 4
        qT = place("qT", [P, KA, NT], where=o_qkv)
        kT = place("kT", [P, KA, NT], where=o_qkv + B_ACT8)
        vT = place("vT", [P, KA, NT], where=o_qkv + 2 * B_ACT8)
        yT = place("yT", [P, KC, NT], where=o_qkv + 3 * B_ACT8)
        tail = o_qkv + 4 * B_ACT8
        sq4 = place("sq4", [P, SK, NT], where=tail)
        x_rows = place("x_rows", [P, 3, D], where=off_split)
        c_rows = place("c_rows", [NC, D], where=off_split + 3 * D * 4)
        c_sig = place("c_sig", [NC, D], where=off_act)
        vec_rows = place("vec_rows", [4 * KT + CW * KC, P], where=off_act + D * 4)
        b_rows = place("b_rows", [NMOD * KT, P], where=off_act + D * 4 + 512)
        st_rows = place("st_rows", [SB * 2, DC], where=off_act + D * 4 + 1024)
        xn = place("xn", [P, KT, NT], where=o_qkv)
        o = o_qkv
        z_p = place("z_p", [P, KC, CW - 1 + TP], where=o); o += KC * (CW - 1 + TP) * 4
        z_s = place("z_s", [P, KC, SB, CW - 1 + ST], where=o); o += KC * SB * (CW - 1 + ST) * 4
        u_t = place("u_t", [P, MT, NT], where=o); o += MT * NT * 4
        conv = place("conv", [P, MT, NT], where=o); o += MT * NT * 4
        o = o_qkv + 20480
        lfz = place("lfz", [H, NT], where=o); o += NT * 4
        lfe = place("lfe", [H, NT], where=o); o += NT * 4
        st_T = place("st_T", [P, KC, SB, 2], where=o); o += KC * SB * 2 * 4
        m4_T = place("m4_T", [ST, P], where=o); o += P * 4
        assert o <= o_qkv + 3 * B_ACT8
        o = o_qkv + 3 * B_ACT8
        wf = place("wf", [P, KT, H], where=o); o += KT * H * 4
        wf_hi = place("wf_hi", [P, KT, H], F32R, where=o); o += KT * H * 4
        wf_lo = place("wf_lo", [P, KT, H], F32R, where=o); o += KT * H * 4
        z_end = place("z_end", [P, KC, 2 + 2 * SB], where=tail)
        z_rows = place("z_rows", [2 + 2 * SB, DC], where=tail + 576)
        assert tail + 576 + DC * 4 <= top
        o_hi = place("o_hi", [P, KA, NT], F32R, where=R)
        o_lo = place("o_lo", [P, KA, NT], F32R, where=R + B_ACT8)
        k_rows = place("k_rows", [P, 3, DA], where=R)
        w = R + 2 * B_ACT8
        cumk = place("cumk", [48, SB, PAST + TS], where=w); w += SB * (PAST + TS) * 4
        q_st = [place(f"q_st{j}", [112, TP], where=w + j * TP * 4) for j in range(2)]; w += 2 * TP * 4
        q_bd = place("q_bd", [P, KA, 32], where=w); w += KA * 32 * 4
        w_end1 = w
        assert w <= o_qkv, (w, o_qkv)
        w = off_split
        KTs = place("KTs", [P, KA, PAST + TS], where=w); w += KA * (PAST + TS) * 4
        v_rows = place("v_rows", [P, 3, DA], where=w); w += 3 * DA * 4
        upto = place("upto", [P, TP], where=w)
        after = place("after", [P, P], where=w + TP * 4)
        pT_s = place("pT_s", [P, 2, 3 * P], where=w); w += 6 * P * 4
        pT_p = place("pT_p", [P, 3 * P], where=w); w += 3 * P * 4
        s_s = place("s_s", [P, 2, PAST + TS], where=w); w += 2 * (PAST + TS) * 4
        v_st = place("v_st", [P, 2, P], where=w); w += 2 * P * 4
        cumk_s = place("cumk_s", [48, PAST + TS], where=w); w += (PAST + TS) * 4
        assert w <= off_split + 2 * SPLIT * SK * SN * 4, w - off_split
        w = tail
        s_p = [place(f"s_p{j}", [P, 3 * P], where=w + j * 3 * P * 4) for j in range(2)]; w += 6 * P * 4
        o_s = place("o_s", [P, 2, P], where=w); w += 2 * P * 4
        w_end2 = w
        k_st = [place(f"k_st{j}", [112, TP], where=w_end1 + j * TP * 4) for j in range(2)]
        assert w_end1 + 2 * TP * 4 <= o_qkv, (w_end1 + 2 * TP * 4, o_qkv)
        assert w_end2 <= top
        y_hi = place("y_hi", [P, KC, NT], F32R, where=o_qkv)
        y_lo = place("y_lo", [P, KC, NT], F32R, where=o_qkv + B_ACT8)
        m_T = place("m_T", [P, KT, NT], where=o_qkv + 2 * B_ACT8)
        gate_a = place("gate_a", [P, MT, NT], where=R + 2 * B_ACT8)
        gate_b = place("gate_b", [P, MT, NT], where=R + 2 * B_ACT8 + MT * NT * 4)
        r_T = place("r_T", [P, KT, NT], where=R)
        hid = place("hid", [P, KF, NT], where=R)
        f_T = place("f_T", [P, KT, NT], where=R + KF * NT * 4)
        assert KF * NT * 4 + KT * NT * 4 <= tail - R
        sg = place("sg", [P, MT, NT], where=tail)
        y_rows = place("y_rows", [P, 3, D], where=R)

        bank = [ctx.enter_context(nc.psum_tensor(f"bank{b}", [P, 512], F32)) for b in range(8)]

        s_c, s_rows, s_x, s_wf, s_table, s_lfc = (sem(n) for n in (
            "c_in", "rows_in", "x_in", "wf_in", "table_in", "lfc_in"))
        raw_full = [sem(f"raw_full{s}") for s in range(RAW)]
        ada_full = [sem(f"ada_full{s}") for s in range(RAW)]
        s_out, s_kout = sem("out_done"), sem("kout_done")
        raw_turn, mm_turn, ada_turn, bank_turn = (sem(n) for n in (
            "raw_turn", "mm_turn", "ada_turn", "bank_turn"))
        hi_done = sem("hi_done")
        act_hi, act_lo = sem("act_hi"), sem("act_lo")
        consts, c_sigm, c_silu, cT_ps, cT_ready = (sem(n) for n in (
            "consts", "c_sigm", "c_silu", "cT_ps", "cT_ready"))
        rows_ps, vec_ready, x_ps = sem("rows_ps"), sem("vec_ready"), sem("x_ps")
        ada_acc, ada_copied, ada_T, ada_mods = (sem(n) for n in (
            "ada_acc", "ada_copied", "ada_T", "ada_mods"))
        sq_done, sqr_done, ms_ps, ms_done, root_done, x1_done, f_done = (sem(n) for n in (
            "sq_done", "sqr_done", "ms_ps", "ms_done", "root_done", "x1_done", "f_done"))
        x_upd = sem("x_upd")
        u_done, gate_done = sem("u_done"), sem("gate_done")
        f_ps, f_z, f_ln, f_lf, lfr_ps, lfr_done, cum_ps, cum_done = (sem(n) for n in (
            "f_ps", "f_z", "f_ln", "f_lf", "lfr_ps", "lfr_done", "cum_ps", "cum_done"))
        wf_hi_done, wf_split = sem("wf_hi_done"), sem("wf_split")
        s_zout, m4_ps, m4_done = sem("zout_done"), sem("m4_ps"), sem("m4_done")
        fixed, pool_sel, sums_ready = sem("fixed"), sem("pool_sel"), sem("sums_ready")
        z_ready, z_ps, z_out = sem("z_ready"), sem("z_ps"), sem("z_out")
        rowT_ps, rowT_out, suf_ps, suf_done, sufT_ps, sufT_done = (sem(n) for n in (
            "rowT_ps", "rowT_out", "suf_ps", "suf_done", "sufT_ps", "sufT_done"))
        q_ready, k_ready, qe_ready, v_ready, S_ps, S_max, S_exp, S_norm, PT_ps, PT_out, O_ps, O_hi, O_lo = (
            sem(n) for n in ("q_ready", "k_ready", "qe_ready", "v_ready", "S_ps", "S_max", "S_exp",
                             "S_norm", "PT_ps", "PT_out", "O_ps", "O_hi", "O_lo"))
        sK_ps, sK_a, sK_d, sQ, sSel, sS_ps, sS_max, sS_exp, sS_norm, sP_ps, sP_out, sO_ps, sO_sb, sOT, sO_hi, sO_lo = (
            sem(n) for n in ("sK_ps", "sK_a", "sK_d", "sQ", "sSel", "sS_ps", "sS_max", "sS_exp", "sS_norm",
                             "sP_ps", "sP_out", "sO_ps", "sO_sb", "sOT", "sO_hi", "sO_lo"))
        page_used = sem("page_used")
        y_ps, y_out = sem("y_ps"), sem("y_out")
        own_act, own_dve, own_pool, own_sp = sem("own_act"), sem("own_dve"), sem("own_pool"), sem("own_sp")

        def slots(w):
            return w[0].rearrange("(q a p) n -> q p a n", a=SK, p=P)

        wv_ada, wv_in, wv_oa, wv_ob, wv_o, wv_f1, wv_f2 = map(
            slots, (w_ada, w_in, w_oa, w_ob, w_o, w_ffn_in, w_ffn_out))
        half_cols = {"u": CU, "C": CC, "B": CB, "q": CQ, "k": CK, "v": CV}

        block = ctx.enter_context(nc.Block())

        @block.sync
        def _(sp):
            def load_ada(m, s, src):
                sp.wait_ge(ada_turn, m + 1)
                sp.dma_start(ada[s][:, :, :], src).then_inc(ada_full[s], 16)

            def load_w(n, s, src):
                sp.wait_ge(raw_turn, n + 1)
                sp.dma_start(raw[s][:, :, :], src).then_inc(raw_full[s], 16)

            with sp.Fori(0, ADA_FIRST) as g:
                for q in range(SK):
                    load_ada(SK * g + q, q, wv_ada[q, :, :, bass.ds(g * SN, SN)])
            for n0, a0, names in ((N_UCB, ADA_FIRST, "uCB"), (N_QKV, ADA_FIRST + 2 * ADA_PER_HALF, "qkv")):
                with sp.Fori(0, HALVES) as i:
                    for t in range(PER_HALF):
                        col = half_cols[names[t // 4]] + i * SN
                        load_w(n0 + PER_HALF * i + t, t % RAW, wv_in[t % 4, :, :, bass.ds(col, SN)])
                        if t % 3 != 2:
                            for e in range(2):
                                j = 4 * (t // 3) + 2 * (t % 3) + e
                                ga = a0 + ADA_PER_HALF * i + j // 4
                                load_ada(4 * ga + j % 4, j % 4, wv_ada[j % 4, :, :, bass.ds(ga * SN, SN)])
            sp.wait_ge(s_table, 16)
            sp.wait_ge(raw_turn, RAW + N_MIX)
            with sp.Fori(0, PAGE_TURNS) as i:
                for j in range(2):
                    for pg in range(NPG):
                        r = sp.value_load(table[0:1, bass.ds((2 * i + j) * NPG + pg, 1)], min_val=0, max_val=POOL - 1)
                        if j == 0 and pg == 0:
                            sp.wait_ge(page_used, 2 * i + 1)
                        for s, src in ((2 * j, cache_k), (2 * j + 1, cache_v)):
                            sp.dma_start(raw[s][:, 2 * pg:2 * pg + 2, :].rearrange("p a n -> p (a n)"),
                                         src[0, bass.ds(r, 1), :, :, :].rearrange("a p h d -> p (a h d)")
                                         ).then_inc(raw_full[s], 16)
            sp.wait_ge(page_used, SB + 1)
            with sp.Fori(0, MIXES) as i:
                for t in range(PER_MIX):
                    if t < 4:
                        src = wv_in[t, :, :, bass.ds(CGA + i * SN, SN)]
                    elif t < 6:
                        src = wv_oa[t - 4, :, :, bass.ds(i * SN, SN)]
                    elif t < 10:
                        src = wv_in[t - 6, :, :, bass.ds(CGB + i * SN, SN)]
                    else:
                        src = wv_ob[t - 10, :, :, bass.ds(i * SN, SN)]
                    if t in (4, 10):
                        sp.wait_ge(raw_turn, N_MIX + PER_MIX * i + t + 1)
                        sp.sem_inc(own_sp, 1)
                        sp.dma_start(raw[t % RAW][:, :, :], src).then_inc(raw_full[t % RAW], 16)
                    else:
                        load_w(N_MIX + PER_MIX * i + t, t % RAW, src)
            with sp.Fori(0, MIXES) as i:
                for t in range(PER_O):
                    load_w(N_O + PER_O * i + t, t, wv_o[t, :, :, bass.ds(i * SN, SN)])
            with sp.Fori(0, F1S) as i:
                for t in range(PER_F1):
                    col = (t // 4) * DFF + i * SN
                    load_w(N_F1 + PER_F1 * i + t, t % RAW, wv_f1[t % 4, :, :, bass.ds(col, SN)])
            with sp.Fori(0, 2) as i:
                for t in range(PER_F2):
                    late = {0: 2, 1: 2}.get(t, 0)
                    sp.wait_ge(raw_turn, N_F2 + PER_F2 * i + t + 1 + late)
                    sp.dma_start(raw[t % RAW][:, :, :],
                                 wv_f2[t % (KF // SK), :, :, bass.ds((2 * i + t // (KF // SK)) * SN, SN)]
                                 ).then_inc(raw_full[t % RAW], 16)

        @block.tensor
        def _(pe):
            def product(n, first, last, G, kt0, hi, lo, buf):
                pe.wait_ge(raw_turn, RAW + n + 1)
                for mt in range(MT):
                    if first:
                        pe.wait_ge(bank_turn, BT + MT * G + mt + 1)
                    cols = slice(mt * P, mt * P + P)
                    for a in range(SK):
                        acc, kt = bank[mt][:, 0:NT], kt0 + a
                        pe.matmul(acc, w_hi[buf][:, a, cols], lo[:, kt, :], start=first and a == 0, stop=False)
                        pe.matmul(acc, w_hi[buf][:, a, cols], hi[:, kt, :], start=False, stop=False)
                        mm = pe.matmul(acc, w_lo[buf][:, a, cols], hi[:, kt, :], start=False,
                                       stop=last and a == SK - 1)
                    mm.then_inc(mm_turn, 1)

            def ada_slot(m, s, q, use):
                pe.wait_ge(ada_full[s], 16 * use)
                for a in range(SK):
                    mm = pe.matmul(bank[4][32 * a:32 * a + 32, :], cT[:, SK * q + a, :], ada[s][:, a, :],
                                   start=q == 0, stop=q == SK - 1, tile_position=(0, 32 * a))
                mm.then_inc(ada_turn, 1)

            def ada_transpose(g):
                pe.wait_ge(ada_copied, g + 2)
                pe.wait_ge(ada_mods, g + 1)
                for m in range(MT):
                    mm = pe.transpose(bank[5][:, m * P:m * P + P], ada_sb[:, m * P:m * P + P], ident[:, :])
                mm.then_inc(ada_T, 1)

            pe.sem_inc(mm_turn, MT * SPLIT)
            pe.sem_inc(ada_turn, RAW)
            pe.sem_inc(ada_T, 1)
            pe.sem_inc(page_used, 1)
            pe.sem_inc(sS_ps, 1)
            pe.sem_inc(O_ps, 1)
            pe.sem_inc(sOT, 1)
            pe.wait_ge(consts, 1)
            pe.transpose(bank[7][:, 0:ST], m4_T[:, :], ident[0:ST, 0:ST]).then_inc(m4_ps, 1)
            pe.wait_ge(s_rows, 16 * 8)
            nv, nb = 4 * KT + CW * KC, NMOD * KT
            pe.transpose(bank[4][:, 0:nv], vec_rows[:, :], ident[0:nv, 0:nv])
            pe.transpose(bank[4][:, P:P + nb], b_rows[:, :], ident[0:nb, 0:nb])
            for kt in range(KC):
                mm = pe.transpose(bank[5][:, 2 * SB * kt:2 * SB * (kt + 1)], st_rows[:, kt * P:kt * P + P],
                                  ident[0:2 * SB, 0:2 * SB])
            mm.then_inc(rows_ps, 1)
            pe.wait_ge(c_silu, 1)
            for kt in range(KT):
                mm = pe.transpose(bank[6][:, NC * kt:NC * (kt + 1)], c_rows[:, kt * P:kt * P + P], ident[0:NC, 0:NC])
            mm.then_inc(cT_ps, 1)
            pe.wait_ge(s_x, 48)
            for kt in range(KT):
                if kt >= 4:
                    pe.wait_ge(bank_turn, kt - 4 + 1)
                for b in range(3):
                    rows = min(P, NT - b * P)
                    mm = pe.transpose(bank[kt % 4][:, b * P:b * P + rows], x_rows[0:rows, b, kt * P:kt * P + P],
                                      ident[0:rows, 0:rows])
                mm.then_inc(x_ps, 1)

            def sum_squares(c, n):
                pe.wait_ge(sqr_done, n)
                pe.matmul(bank[7][:, 0:NT], ones[:, 0:P], sqr[:, :], start=c == 0, stop=c == 3).then_inc(ms_ps, 1)

            pe.wait_ge(m4_done, 1)
            pe.wait_ge(consts, 2)
            for c in range(4):
                sum_squares(c, c + 1)
            pe.wait_ge(cT_ready, 1)
            pe.wait_ge(vec_ready, 1)
            with pe.Fori(0, ADA_FIRST) as g:
                pe.wait_ge(ada_copied, g + 1)
                for q in range(SK):
                    ada_slot(SK * g + q, q, q, g + 1)
                ada_transpose(g)
            pe.wait_ge(wf_split, 1)
            for c in range(4):
                pe.wait_ge(act_lo, c + 1)
                for a in range(SK):
                    kt = SK * c + a
                    acc = bank[6][0:H, 0:NT]
                    pe.matmul(acc, wf_hi[:, kt, :], a_lo[:, kt, :], start=kt == 0, stop=False)
                    pe.matmul(acc, wf_hi[:, kt, :], a_hi[:, kt, :], start=False, stop=False)
                    mm = pe.matmul(acc, wf_lo[:, kt, :], a_hi[:, kt, :], start=False, stop=kt == KT - 1)
            mm.then_inc(f_ps, 1)
            for n0, g0, a0, names in ((N_UCB, G_UCB, ADA_FIRST, "uCB"),
                                      (N_QKV, G_QKV, ADA_FIRST + 2 * ADA_PER_HALF, "qkv")):
                with pe.Fori(0, HALVES) as i:
                    for t in range(PER_HALF):
                        product(n0 + PER_HALF * i + t, t % 4 == 0, t % 4 == 3, g0 + 3 * i + t // 4,
                                SK * (t % 4), a_hi, a_lo, t % SPLIT)
                        ga = a0 + ADA_PER_HALF * i + t // 3
                        if t % 3 != 2:
                            if t % 3 == 0:
                                pe.wait_ge(ada_copied, ga + 1)
                            for e in range(2):
                                q = 2 * (t % 3) + e
                                ada_slot(None, q, q, ga + 1)
                        else:
                            ada_transpose(ga)
                if names == "uCB":
                    pe.wait_ge(z_ready, 1)
                    pe.wait_ge(f_z, 1)
                    for kt in range(KC):
                        mm = pe.transpose(bank[6 + kt // 4][0:2 + 2 * SB, (kt % 4) * P:(kt % 4) * P + P],
                                          z_end[:, kt, :], ident[:, :])
                    mm.then_inc(z_ps, 1)

            pe.wait_ge(f_lf, 1)
            pe.wait_ge(z_out, 1)
            for b in range(3):
                rows = min(P, NT - b * P)
                mm = pe.transpose(bank[6][0:rows, H * b:H * b + H], lf[:, b * P:b * P + rows], ident[0:H, 0:H])
            mm.then_inc(lfr_ps, 1)
            pe.wait_ge(lfr_done, 1)
            pe.wait_ge(sums_ready, 1)
            for p0 in (64, 96):
                acc = bank[7][p0:p0 + H, :]
                pe.matmul(acc[:, 0:TP], lfr[:, 0, :], upto[:, :], start=True, stop=False, tile_position=(0, p0))
                mm = pe.matmul(acc[:, P:TP], lfr[:, 1, :], upto[:, 0:P], start=False, stop=True, tile_position=(0, p0))
            mm.then_inc(cum_ps, 1)
            pe.wait_ge(bank_turn, BT + MT * (G_MIX + 1))
            pe.wait_ge(ada_mods, ADA_G + 1)
            n = 0
            for src in (kT, vT):
                for b in range(3):
                    rows = min(P, NT - b * P)
                    for half in range(2):
                        if n >= 2:
                            pe.wait_ge(rowT_out, n - 1)
                        for j in range(4):
                            mm = pe.transpose(bank[4 + n % 2][0:rows, j * P:j * P + P],
                                              src[:, 4 * half + j, b * P:b * P + rows], ident[:, :])
                        mm.then_inc(rowT_ps, 1)
                        n += 1
            pe.wait_ge(s_lfc, 16 * SB * NPG)
            pe.wait_ge(lfr_done, 1)
            pages = lfc[:, :, :, :]
            acc = bank[6][:, 0:SB * NPG * H].rearrange("p (s g h) -> p s g h", s=SB, g=NPG)
            pe.matmul(acc, after[:, :], pages, start=True, stop=False)
            pe.matmul(acc[:, :, 0, :], ones[:, 0:P], pages[:, :, 1, :], start=False, stop=True).then_inc(suf_ps, 1)
            pe.wait_ge(suf_done, 1)
            pe.wait_ge(rowT_out, 12)
            for s in range(SB):
                for pg in range(NPG):
                    b = s // 2
                    mm = pe.transpose(bank[b][0:H, (s % 2) * PAST + pg * P:(s % 2) * PAST + pg * P + P],
                                      suf[:, s, pg, :], ident[:, :])
            mm.then_inc(sufT_ps, 1)
            pe.wait_ge(sufT_done, 1)
            pe.wait_ge(cum_done, 1)
            pe.wait_ge(fixed, 1)

            def scores(h, j):
                pe.wait_ge(q_ready, h + 1)
                pe.wait_ge(k_ready, h + 1)
                pe.wait_ge(qe_ready, h + 1)
                pe.wait_ge(S_max, h + 1)
                pe.matmul(bank[j][:, 0:P], q_st[j][:, 0:P], k_st[j][:, 0:P], start=True, stop=True)
                pe.matmul(bank[j][:, P:3 * P], q_st[j][:, P:TP], k_st[j][:, :], start=True, stop=True,
                          skip_group_check=True).then_inc(S_ps, 1)

            def prompt_turn(h, j):
                pe.wait_ge(S_norm, h + 1)
                pe.wait_ge(PT_out, h + 1)
                for b in range(3):
                    mm = pe.transpose(bank[2][:, b * P:b * P + P], s_p[j][:, b * P:b * P + P], ident[:, :])
                mm.then_inc(PT_ps, 1)

            def prompt_out(h, j, pair):
                pe.wait_ge(PT_out, h + 2)
                pe.wait_ge(v_ready, pair + 1)
                if j == 0:
                    pe.wait_ge(O_lo, pair + 1)
                acc, c0 = bank[3][DH * j:DH * j + DH, :], DH * j
                pe.matmul(acc[:, 0:TP], v_st[:, 0, c0:c0 + DH], pT_p[:, 0:TP], start=True, stop=False,
                          tile_position=(0, DH * j))
                pe.matmul(acc[:, P:TP], v_st[:, 1, c0:c0 + DH], pT_p[:, TP:3 * P], start=False, stop=True,
                          tile_position=(0, DH * j)).then_inc(O_ps, 1)

            with pe.Fori(0, PAGE_TURNS) as i:
                for j in range(2):
                    s = 2 * i + j
                    kp, vp = raw[2 * j], raw[2 * j + 1]
                    pe.wait_ge(raw_full[2 * j], 16 * (R_PAGES + NPG * (i + 1)))
                    pe.wait_ge(sP_out, s + 1)
                    for n in range(4):
                        if n == 2:
                            pe.wait_ge(sK_a, 2 * s + 1)
                        if n == 3:
                            pe.wait_ge(sK_d, 2 * s + 1)
                        pg, f0 = n // 2, 4 * (n % 2)
                        for f in range(4):
                            ft = f0 + f
                            mm = pe.transpose(bank[4 + n % 2][:, f * P:f * P + P],
                                              kp[:, 2 * pg + ft // 4, (ft % 4) * P:(ft % 4) * P + P], ident[:, :])
                        mm.then_inc(sK_ps, 1)
                    scores(2 * s, 0)
                    pe.wait_ge(sK_a, 2 * s + 2)
                    pe.wait_ge(sK_d, 2 * s + 2)
                    pe.wait_ge(sQ, s + 1)
                    pe.wait_ge(sSel, s + 1)
                    pe.wait_ge(sO_lo, s + 1)
                    for hf in range(2):
                        for q4 in range(4):
                            acc = bank[6 + hf][32 * q4:32 * q4 + 32, 0:PAST + TS]
                            pe.matmul(acc, q_bd[:, 4 * hf + q4, :], KTs[:, 4 * hf + q4, :], start=True, stop=False,
                                      tile_position=(0, 32 * q4))
                        for q4 in range(4):
                            acc = bank[6 + hf][32 * q4:32 * q4 + 32, 0:PAST + TS]
                            mm = pe.matmul(acc, selq[:, 4 * hf + q4, :],
                                           cumk_s[:, :],
                                           start=False, stop=True, tile_position=(0, 32 * q4))
                        mm.then_inc(sS_ps, 1)
                    scores(2 * s + 1, 1)
                    prompt_turn(2 * s, 0)
                    pe.wait_ge(sS_norm, s + 1)
                    for hf in range(2):
                        for pg in range(2):
                            pe.transpose(bank[4 + hf][:, pg * P:pg * P + P], s_s[:, hf, pg * P:pg * P + P], ident[:, :])
                        mm = pe.transpose(bank[4 + hf][0:TS, 2 * P:3 * P], s_s[:, hf, PAST:PAST + TS], ident[:, :])
                    mm.then_inc(sP_ps, 1)
                    prompt_out(2 * s, 0, s)
                    prompt_turn(2 * s + 1, 1)
                    pe.wait_ge(sP_out, s + 2)
                    pe.wait_ge(raw_full[2 * j + 1], 16 * (R_PAGES + NPG * (i + 1)))
                    for hf in range(2):
                        for blk in range(3):
                            for q4 in range(4):
                                acc = bank[6][32 * q4:32 * q4 + 32, hf * P:hf * P + P]
                                ft = 4 * hf + q4
                                if blk < 2:
                                    lhs = pT_s[:, hf, blk * P + 32 * q4:blk * P + 32 * q4 + 32]
                                    rhs = vp[:, 2 * blk + ft // 4, (ft % 4) * P:(ft % 4) * P + P]
                                else:
                                    lhs = pT_s[0:TS, hf, 2 * P + 32 * q4:2 * P + 32 * q4 + 32]
                                    rhs = v_rows[0:TS, 2, ft * P:ft * P + P]
                                mm = pe.matmul(acc, lhs, rhs, start=blk == 0, stop=blk == 2,
                                               tile_position=(0, 32 * q4), skip_group_check=True)
                    mm.then_inc(page_used, 1)
                    prompt_out(2 * s + 1, 1, s)
                    pe.wait_ge(sO_sb, s + 1)
                    for hf in range(2):
                        mm = pe.transpose(bank[7][:, hf * P:hf * P + P], o_s[:, hf, :], ident[:, :])
                    mm.then_inc(sOT, 1)

            pe.wait_ge(O_lo, SB + 1)
            pe.wait_ge(sO_lo, SB + 1)
            with pe.Fori(0, MIXES) as i:
                for t in range(PER_MIX):
                    n = N_MIX + PER_MIX * i + t
                    g = G_MIX + 4 * i
                    if t < 4:
                        product(n, t == 0, t == 3, g, SK * t, a_hi, a_lo, t % SPLIT)
                    elif t < 6:
                        product(n, t == 4, t == 5, g + 1, SK * (t - 4), o_hi, o_lo, t % SPLIT)
                    elif t < 10:
                        product(n, t == 6, t == 9, g + 2, SK * (t - 6), a_hi, a_lo, t % SPLIT)
                    else:
                        if t == 10:
                            pe.wait_ge(act_lo, 4 + 2)
                        product(n, t == 10, t == 11, g + 3, SK * (t - 10), y_hi, y_lo, t % SPLIT)
            with pe.Fori(0, MIXES) as i:
                for t in range(PER_O):
                    pe.wait_ge(act_lo, 6 + t + 1)
                    product(N_O + PER_O * i + t, t == 0, t == 3, G_O + i, SK * t, a_hi, a_lo, t % SPLIT)
            for c in range(4):
                sum_squares(c, 4 + c + 1)
            for c in range(4):
                sum_squares(c, 8 + c + 1)
            with pe.Fori(0, F1S) as i:
                for t in range(PER_F1):
                    pe.wait_ge(act_lo, 10 + t % 4 + 1)
                    product(N_F1 + PER_F1 * i + t, t % 4 == 0, t % 4 == 3, G_F1 + 2 * i + t // 4,
                            SK * (t % 4), a_hi, a_lo, t % SPLIT)
            with pe.Fori(0, 2) as i:
                for t in range(PER_F2):
                    k = KF // SK
                    pe.wait_ge(act_lo, 14 + PER_F2 * i + t + 1)
                    product(N_F2 + PER_F2 * i + t, t % k == 0, t % k == k - 1, G_F2 + 2 * i + t // k,
                            SK * (t % 4), a_hi, a_lo, t % SPLIT)
            for c in range(4):
                sum_squares(c, 12 + c + 1)
            n = 0
            for c in range(4):
                pe.wait_ge(x_upd, 4 + c + 1)
                for b in range(3):
                    rows = min(P, NT - b * P)
                    if n >= 4:
                        pe.wait_ge(y_out, n - 3)
                    for j in range(4):
                        mm = pe.transpose(bank[n % 4][0:rows, j * P:j * P + P],
                                          xT[:, 4 * c + j, b * P:b * P + rows], ident[:, :])
                    mm.then_inc(y_ps, 1)
                    n += 1

        @block.scalar
        def _(act):
            own = Own(act, own_act)
            act.sem_inc(ada_copied, 1)
            act.sem_inc(sP_out, 1)
            act.sem_inc(PT_out, 1)

            def split_hi(n, s, use, buf):
                act.wait_ge(raw_full[s], 16 * use)
                act.wait_ge(mm_turn, MT * n + MT)
                nc.scalar.copy(w_hi[buf][:, :, :], raw[s][:, :, :]).then_inc(hi_done, 1)

            def groups_done(n, mt):
                act.wait_ge(mm_turn, MT * SPLIT + MT * n + mt + 1)

            act.dma_start(c_rows[0:1, :], c_prompt).then_inc(s_c, 16)
            act.dma_start(c_rows[1:NC, :], c_sample).then_inc(s_c, 16)
            for n, g in enumerate((g_pre1, g_post1, g_pre2, g_post2)):
                act.dma_start(vec_rows[KT * n:KT * n + KT, :], g[0].rearrange("(k p) -> k p", p=P)).then_inc(s_rows, 16)
            act.dma_start(vec_rows[4 * KT:4 * KT + CW * KC, :],
                          w_conv[0].rearrange("c (k p) -> (c k) p", p=P)).then_inc(s_rows, 16)
            act.dma_start(b_rows[:, :], b_ada[0].rearrange("(k p) -> k p", p=P)).then_inc(s_rows, 16)
            act.dma_start(st_rows[:, :], state_conv[0].rearrange("s t n -> (s t) n")).then_inc(s_rows, 16)
            act.dma_start(bf[:, :], b_f[0].rearrange("(h a) -> h a", a=1)).then_inc(s_rows, 16)
            for b in range(2):
                act.dma_start(x_rows[:, b, :], x_prompt[0, b * P:b * P + P, :]).then_inc(s_x, 16)
            act.dma_start(x_rows[0:TS, 2, :], x_sample.rearrange("s t n -> (s t) n")).then_inc(s_x, 16)
            act.dma_start(table[0:1, :], page_table.rearrange("(a s) g -> a (s g)", a=1)).then_inc(s_table, 16)
            act.dma_start(wf[:, :, :], w_in[0, :, CF:CF + H].rearrange("(k p) n -> p k n", p=P)).then_inc(s_wf, 16)

            act.wait_ge(s_c, 32)
            nc.scalar.activation(c_sig[:, :], c_rows[:, :], ACT.Sigmoid).then_inc(c_sigm, 1)

            def squares(src, c, n):
                if n:
                    act.wait_ge(sqr_done, n)
                nc.scalar.activation(sq4[:, :, :], src[:, SK * c:SK * c + SK, :], ACT.Square).then_inc(sq_done, 1)

            for c in range(4):
                act.wait_ge(bank_turn, SK * c + SK)
                squares(xT, c, c)
            act.wait_ge(ms_done, 1)
            nc.scalar.activation(rstd[:, :], rstd[:, :], ACT.Sqrt).then_inc(root_done, 1)
            act.wait_ge(s_wf, 16)
            nc.scalar.copy(wf_hi[:, :, :], wf[:, :, :]).then_inc(wf_hi_done, 1)

            def copy_ada(g):
                act.wait_ge(ada_turn, RAW + SK * g + SK)
                act.wait_ge(ada_T, g + 1)
                nc.scalar.copy(ada_sb[:, :], bank[4][:, :]).then_inc(ada_copied, 1)

            with act.Fori(0, ADA_FIRST) as g:
                copy_ada(g)

            def split_act(src, kt, dst, kd, tiles=SK):
                nc.scalar.copy(dst[:, kd:kd + tiles, :], src[:, bass.ds(kt, tiles), :]).then_inc(act_hi, 1)

            for c in range(4):
                act.wait_ge(x_upd, c + 1)
                split_act(xn, SK * c, a_hi, SK * c)
            act.wait_ge(f_z, 1)
            own.mark(nc.scalar.activation(lfe[:, :], lfe[:, :], ACT.Exp))
            own.wait()
            nc.scalar.activation(lfe[:, :], lfe[:, :], ACT.Ln, bias=1.0).then_inc(f_ln, 1)

            def half_body(i, n0, names, a0, more):
                for t in range(PER_HALF):
                    if t < PER_HALF - 1 or more:
                        split_hi(n0 + PER_HALF * i + t + 1, (t + 1) % RAW, n0 // RAW + 3 * i + (t + 1) // RAW + 1,
                                 (t + 1) % SPLIT)
                    name = names[t // 4]
                    if t % 4 == 3 and name in "uqkv":
                        dst = {"u": u_t, "q": qT, "k": kT, "v": vT}[name]
                        for mt in range(MT):
                            groups_done(n0 + PER_HALF * i + t, mt)
                            kt = mt if name == "u" else 4 * i + mt
                            nc.scalar.copy(dst[:, bass.ds(kt, 1), :].rearrange("p a n -> p (a n)"),
                                           bank[mt][:, 0:NT]).then_inc(bank_turn, 1)
                    if t % 3 == 1:
                        copy_ada(a0 + ADA_PER_HALF * i + t // 3)

            act.wait_ge(x_ps, KT)
            split_hi(0, 0, 1, 0)
            with act.Fori(0, HALVES) as i:
                half_body(i, N_UCB, "uCB", ADA_FIRST, True)
            for i in range(HALVES):
                half_body(i, N_QKV, "qkv", ADA_FIRST + 2 * ADA_PER_HALF, i < HALVES - 1)

            n = 0
            for dst in (k_rows, v_rows):
                for b in range(3):
                    rows = min(P, NT - b * P)
                    for half in range(2):
                        act.wait_ge(rowT_ps, n + 1)
                        nc.scalar.copy(dst[0:rows, b, half * 512:half * 512 + 512],
                                       bank[4 + n % 2][0:rows, :]).then_inc(rowT_out, 1)
                        n += 1
            nc.scalar.copy(KTs[:, :, PAST:PAST + TS], kT[:, :, TP:NT])
            act.wait_ge(sufT_ps, 1)
            act.wait_ge(fixed, 1)
            for b in range(4):
                ins = nc.scalar.copy(cumk[0:H, 2 * b:2 * b + 2, 0:PAST],
                                     bank[b][0:H, :].rearrange("p (s n) -> p s n", s=2))
            ins.then_inc(sufT_done, 1)
            act.wait_ge(s_kout, 32)

            def copy_q(pair, j):
                h = 2 * pair + j
                act.wait_ge(S_max, h + 1)
                nc.scalar.mul(q_st[j][0:DH, :], qT[DH * j:DH * j + DH, bass.ds(pair, 1), 0:TP].rearrange(
                    "p a n -> p (a n)"), SCALE).then_inc(q_ready, 1)

            def exp_head(h, j):
                act.wait_ge(S_max, h + 3)
                nc.scalar.activation(s_p[j][:, 0:P], s_p[j][:, 0:P], ACT.Exp, bias=small[:, 4 * j:4 * j + 1],
                                     accum_out=small[:, 4 * j + 2:4 * j + 3])
                nc.scalar.activation(s_p[j][:, P:3 * P], s_p[j][:, P:3 * P], ACT.Exp,
                                     bias=small[:, 4 * j + 1:4 * j + 2],
                                     accum_out=small[:, 4 * j + 3:4 * j + 4]).then_inc(S_exp, 1)

            def copy_pT(h):
                act.wait_ge(PT_ps, h + 1)
                act.wait_ge(O_ps, h + 1)
                nc.scalar.copy(pT_p[:, :], bank[2][:, 0:3 * P]).then_inc(PT_out, 1)

            with act.Fori(0, PAGE_TURNS) as i:
                for j in range(2):
                    s = 2 * i + j
                    copy_q(s, 0)
                    act.wait_ge(sS_ps, 2 * s + 1)
                    tok = bass.ds(TP + ST * s, ST)
                    nc.scalar.mul(q_bd[0:DH, :, 0:ST], qT[0:DH, :, tok], SCALE)
                    nc.scalar.mul(q_bd[DH:P, :, ST:2 * ST], qT[DH:P, :, tok], SCALE).then_inc(sQ, 1)
                    for n in (0, 2):
                        act.wait_ge(sK_ps, 4 * s + n + 1)
                        if n == 0:
                            act.wait_ge(sS_ps, 2 * s + 1)
                        nc.scalar.copy(KTs[:, 0:4, (n // 2) * P:(n // 2) * P + P],
                                       bank[4][:, :].rearrange("p (f n) -> p f n", f=4)).then_inc(sK_a, 1)
                    copy_q(s, 1)
                    exp_head(2 * s, 0)
                    act.wait_ge(sS_max, s + 1)
                    nc.scalar.activation(s_s[:, 0, :], s_s[:, 0, :], ACT.Exp, bias=small[:, 8:9],
                                         accum_out=small[:, 10:11])
                    nc.scalar.activation(s_s[:, 1, :], s_s[:, 1, :], ACT.Exp, bias=small[:, 9:10],
                                         accum_out=small[:, 11:12]).then_inc(sS_exp, 1)
                    exp_head(2 * s + 1, 1)
                    copy_pT(2 * s)
                    act.wait_ge(sP_ps, s + 1)
                    act.wait_ge(page_used, s + 1)
                    for hf in range(2):
                        nc.scalar.copy(pT_s[:, hf, 0:2 * P], bank[4 + hf][:, 0:2 * P])
                        ins = nc.scalar.copy(pT_s[0:TS, hf, 2 * P:3 * P], bank[4 + hf][0:TS, 2 * P:3 * P])
                    ins.then_inc(sP_out, 1)
                    copy_pT(2 * s + 1)
                    act.wait_ge(page_used, s + 2)
                    act.wait_ge(sOT, s + 1)
                    nc.scalar.copy(o_s[:, :, :], bank[6][:, 0:2 * P].rearrange("p (a n) -> p a n", a=2)).then_inc(sO_sb, 1)
                    act.wait_ge(O_ps, 2 * s + 3)
                    nc.scalar.copy(o_hi[:, bass.ds(s, 1), 0:TP].rearrange("p a n -> p (a n)"),
                                   bank[3][:, 0:TP]).then_inc(O_hi, 1)
                    act.wait_ge(sOT, s + 2)
                    for e in range(2):
                        src = bank[7][DH * e:DH * e + DH, 0:2 * P].rearrange("p (k c) -> p k c", c=32)
                        ins = nc.scalar.copy(o_hi[DH * e:DH * e + DH, :, tok], src[:, :, ST * e:ST * e + ST])
                    ins.then_inc(sO_hi, 1)

            act.wait_ge(O_lo, SB + 1)
            act.wait_ge(sO_lo, SB + 1)
            act.wait_ge(sOT, SB + 1)
            act.wait_ge(s_out, 16 * 5)
            split_hi(N_MIX, 0, R_MIX + 1, 0)
            for c in range(2):
                split_act(yT, SK * c, y_hi, SK * c)
            with act.Fori(0, MIXES) as i:
                for t in range(PER_MIX):
                    n = N_MIX + PER_MIX * i + t
                    split_hi(n + 1, (t + 1) % RAW, R_MIX + 3 * i + (t + 1) // RAW + 1, (t + 1) % SPLIT)
                    if t in (3, 9):
                        for mt in range(MT):
                            groups_done(n, mt)
                            nc.scalar.activation((gate_a if t == 3 else gate_b)[:, mt, :], bank[mt][:, 0:NT],
                                                 ACT.Sigmoid).then_inc(bank_turn, 1)
            act.wait_ge(mm_turn, MT * (SPLIT + N_O))
            for c in range(4):
                act.wait_ge(bank_turn, BT + MT * (G_O + 1))
                split_act(m_T, SK * c, a_hi, SK * c)
            with act.Fori(0, MIXES) as i:
                for t in range(PER_O):
                    split_hi(N_O + PER_O * i + t + 1, (t + 1) % RAW, R_O + i + (t + 1) // RAW + 1, (t + 1) % SPLIT)
                for mt in range(MT):
                    groups_done(N_O + PER_O * i + PER_O - 1, mt)
                    nc.scalar.copy(r_T[:, bass.ds(MT * i + mt, 1), :].rearrange("p a n -> p (a n)"),
                                   bank[mt][:, 0:NT]).then_inc(bank_turn, 1)
            act.wait_ge(bank_turn, BT + MT * (G_F1 + 1))
            for c in range(4):
                squares(r_T, c, 4 + c)
            act.wait_ge(ms_done, 2)
            nc.scalar.activation(rstd[:, :], rstd[:, :], ACT.Sqrt).then_inc(root_done, 1)
            for c in range(4):
                act.wait_ge(x1_done, c + 1)
                squares(xT, c, 8 + c)
            act.wait_ge(ms_done, 3)
            nc.scalar.activation(rstd[:, :], rstd[:, :], ACT.Sqrt).then_inc(root_done, 1)
            for c in range(4):
                act.wait_ge(f_done, c + 1)
                split_act(r_T, SK * c, a_hi, SK * c)
            with act.Fori(0, F1S) as i:
                for t in range(PER_F1):
                    n = N_F1 + PER_F1 * i + t
                    split_hi(n + 1, (t + 1) % RAW, R_F1 + 2 * i + (t + 1) // RAW + 1, (t + 1) % SPLIT)
                    if t == 3:
                        act.wait_ge(bank_turn, BT + MT * (G_F1 + 2 * i + 1))
                        for mt in range(MT):
                            groups_done(n, mt)
                            nc.scalar.activation(sg[:, mt, :], bank[mt][:, 0:NT], ACT.Sigmoid).then_inc(gate_done, 1)
            k = KF // SK
            act.wait_ge(bank_turn, BT + MT * (G_F2 + 1))
            for c in range(2):
                split_act(hid, SK * c, a_hi, SK * c)

            def f2_body(i, more):
                for t in range(PER_F2):
                    n = N_F2 + PER_F2 * i + t
                    if t < PER_F2 - 1:
                        split_hi(n + 1, (t + 1) % RAW, R_F2 + [6, 6, 5, 5][(t + 1) % RAW] * i + (t + 1) // RAW + 1,
                                 (t + 1) % SPLIT)
                    elif more:
                        split_hi(n + 1, 0, R_F2 + 6 * (i + 1) + 1, 0)
                    if t % k == k - 1:
                        for mt in range(MT):
                            groups_done(n, mt)
                            nc.scalar.copy(f_T[:, bass.ds(MT * (2 * i + t // k) + mt, 1), :].rearrange("p a n -> p (a n)"),
                                           bank[mt][:, 0:NT]).then_inc(bank_turn, 1)
                    if t < PER_F2 - 2 or more:
                        t2 = (t + 2) % PER_F2
                        last = n - 2 if t + 2 < PER_F2 else N_F2 + PER_F2 * i + 20 + t2
                        act.wait_ge(mm_turn, MT * (SPLIT + last + 1))
                        split_act(hid, SK * (t2 % k), a_hi, SK * (t2 % 4))

            for i in range(2):
                f2_body(i, i == 0)
            act.wait_ge(bank_turn, BT + MT * (G_END + 1))
            for c in range(4):
                squares(f_T, c, 12 + c)
            act.wait_ge(ms_done, 4)
            nc.scalar.activation(rstd[:, :], rstd[:, :], ACT.Sqrt).then_inc(root_done, 1)
            n = 0
            for c in range(4):
                for b in range(3):
                    rows = min(P, NT - b * P)
                    act.wait_ge(y_ps, n + 1)
                    nc.scalar.copy(y_rows[0:rows, b, SN * c:SN * c + SN], bank[n % 4][0:rows, :]).then_inc(y_out, 1)
                    n += 1

        @block.vector
        def _(dve):
            own = Own(dve, own_dve)
            tt, ts, stt = nc.vector.tensor_tensor, nc.vector.tensor_scalar, nc.vector.scalar_tensor_tensor

            def split_lo(n, s, buf):
                dve.wait_ge(hi_done, n + 1)
                tt(w_lo[buf][:, :, :], raw[s][:, :, :], w_hi[buf][:, :, :].bitcast(F32),
                   ALU.subtract).then_inc(raw_turn, 1)

            def groups_done(n, mt):
                dve.wait_ge(mm_turn, MT * SPLIT + MT * n + mt + 1)

            def seqs(ap, kts):
                return ap.rearrange("p k (s t) -> p k s t", s=SB)

            def cond(tile, k0, kts):
                return tile[:, k0:k0 + kts, 1:NC].unsqueeze(3).broadcast_to([P, kts, SB, ST])

            dve.sem_inc(raw_turn, RAW)
            dve.sem_inc(ada_mods, 1)
            dve.sem_inc(S_max, 2)
            dve.sem_inc(O_lo, 1)
            dve.sem_inc(sO_lo, 1)
            own.mark(nc.vector.memset(cT[:, :, :], 0.0))
            dve.wait_ge(c_sigm, 1)
            tt(c_rows[:, :], c_rows[:, :], c_sig[:, :], ALU.mult).then_inc(c_silu, 1)
            dve.wait_ge(rows_ps, 1)
            nv, nb = 4 * KT + CW * KC, NMOD * KT
            own.mark(nc.vector.tensor_copy(vecT[:, :], bank[4][:, 0:nv]))
            own.mark(nc.vector.tensor_copy(bT[:, :], bank[4][:, P:P + nb]))
            nc.vector.tensor_copy(st_T[:, :, :, :], bank[5][:, 0:KC * SB * 2].rearrange(
                "p (k s t) -> p k s t", k=KC, s=SB)).then_inc(vec_ready, 1)
            dve.wait_ge(m4_ps, 1)
            own.mark(nc.vector.memset(mask_s[:, :], MASKED))
            own.wait()
            nc.vector.tensor_copy(mask_s[:, :].rearrange("p (s c) -> p s c", s=SB)[:, :, 0:ST],
                                  bank[7][:, 0:ST].unsqueeze(1).broadcast_to([P, SB, ST])).then_inc(m4_done, 1)
            dve.wait_ge(consts, 3)
            own.mark(nc.vector.tensor_copy(sel[32:32 + H, :, :], sel[0:H, :, :]))
            own.wait()
            nc.vector.tensor_copy(selq[:, :, 0:2 * ST], sel[:, :, :]).then_inc(pool_sel, 1)
            dve.wait_ge(cT_ps, 1)
            own.wait()
            nc.vector.tensor_copy(cT[:, :, 0:NC], bank[6][:, 0:KT * NC].rearrange("p (k r) -> p k r", k=KT)
                                  ).then_inc(cT_ready, 1)
            for kt in range(KT):
                dve.wait_ge(x_ps, kt + 1)
                nc.vector.tensor_copy(xT[:, kt, :], bank[kt % 4][:, 0:NT]).then_inc(bank_turn, 1)

            def sum_of_four(n):
                dve.wait_ge(sq_done, n + 1)
                if n:
                    dve.wait_ge(ms_ps, n)
                nc.vector.tensor_reduce(sqr[:, :], sq4[:, :, :].rearrange("p k t -> p t k"), AX.X, ALU.add
                                        ).then_inc(sqr_done, 1)

            def mean_square(n):
                dve.wait_ge(ms_ps, n)
                own.mark(ts(sq4[:, 1, :], bank[7][:, 0:NT], 1.0 / D, EPS, ALU.mult, ALU.add))
                own.wait()
                nc.vector.reciprocal(rstd[:, :], sq4[:, 1, :]).then_inc(ms_done, 1)

            def refine_root(n):
                dve.wait_ge(root_done, n)
                own.mark(tt(sq4[:, 0, :], rstd[:, :], rstd[:, :], ALU.mult))
                own.wait()
                own.mark(stt(sq4[:, 0, :], sq4[:, 0, :], -0.5, sq4[:, 1, :], ALU.mult, ALU.mult))
                own.wait()
                own.mark(stt(rstd[:, :], sq4[:, 0, :], 1.5, rstd[:, :], ALU.add, ALU.mult))
                own.wait()

            def times_rstd(dst, src, c):
                own.mark(tt(dst[:, SK * c:SK * c + SK, :], src[:, SK * c:SK * c + SK, :],
                            rstd[:, :].unsqueeze(1).broadcast_to([P, SK, NT]), ALU.mult))

            def modulate(dst, A, S0, c):
                own.wait()
                k0 = SK * c
                own.mark(tt(seqs(dst[:, k0:k0 + SK, TP:NT], SK), seqs(dst[:, k0:k0 + SK, TP:NT], SK),
                            cond(A, k0, SK), ALU.mult))
                for kt in range(k0, k0 + SK):
                    own.mark(ts(dst[:, kt, 0:TP], dst[:, kt, 0:TP], A[:, kt, 0:1], mods[:, S0 + kt, 0:1],
                                ALU.mult, ALU.add))
                own.wait()
                return tt(seqs(dst[:, k0:k0 + SK, TP:NT], SK), seqs(dst[:, k0:k0 + SK, TP:NT], SK),
                          cond(mods, S0 + k0, SK), ALU.add)

            for c in range(4):
                sum_of_four(c)
            mean_square(4)
            refine_root(1)
            for c in range(4):
                times_rstd(xn, xT, c)
            dve.wait_ge(wf_hi_done, 1)
            tt(wf_lo[:, :, :], wf[:, :, :], wf_hi[:, :, :].bitcast(F32), ALU.subtract).then_inc(wf_split, 1)

            def add_ada(g):
                dve.wait_ge(ada_T, g + 2)
                src = bank[5][:, :].rearrange("p (m j r) -> p m r j", m=MT, j=4)[:, :, 0:NC, :]
                nc.vector.tensor_reduce(mods[:, bass.ds(MT * g, MT), :], src, AX.X, ALU.add).then_inc(ada_mods, 1)

            with dve.Fori(0, ADA_FIRST) as g:
                add_ada(g)

            def add_bias(lo_, hi_):
                own.mark(tt(mods[:, lo_:hi_, :], mods[:, lo_:hi_, :],
                            bT[:, lo_:hi_].unsqueeze(2).broadcast_to([P, hi_ - lo_, NC]), ALU.add))
                own.wait()

            def scaled(dst, g0, part, plus):
                own.mark(stt(dst[:, :, :], mods[:, part * KT:part * KT + KT, :], plus,
                             vecT[:, g0:g0 + KT].unsqueeze(2).broadcast_to([P, KT, NC]), ALU.add, ALU.mult))
                own.wait()

            dve.wait_ge(ada_mods, ADA_FIRST + 1)
            add_bias(0, 2 * KT)
            scaled(modA, 0, 1, 1.0)
            for c in range(4):
                modulate(xn, modA, 0, c).then_inc(x_upd, 1)

            def split_act_lo(n, src, kt, hi, lo, kd):
                dve.wait_ge(act_hi, n + 1)
                tt(lo[:, kd:kd + SK, :], src[:, bass.ds(kt, SK), :], hi[:, kd:kd + SK, :].bitcast(F32),
                   ALU.subtract).then_inc(act_lo, 1)

            for c in range(4):
                split_act_lo(c, xn, SK * c, a_hi, a_lo, SK * c)
            dve.wait_ge(f_ps, 1)
            own.mark(ts(lfz[:, :], bank[6][0:H, 0:NT], bf[:, 0:1], None, ALU.add))
            own.wait()
            own.mark(ts(lfe[:, :], lfz[:, :], -1.0, None, ALU.mult))
            own.wait()
            tt(lfe[:, :], lfe[:, :], lfz[:, :], ALU.min).then_inc(f_z, 1)
            own.mark(nc.vector.memset(z_p[:, :, 0:CW - 1], 0.0))
            own.mark(nc.vector.tensor_copy(z_s[:, :, :, 0:CW - 1],
                                           st_T[:, :, :, :]))
            dve.wait_ge(f_ln, 1)
            stt(lf[:, :], lfz[:, :], 0.0, lfe[:, :], ALU.min, ALU.subtract).then_inc(f_lf, 1)

            def half_body(i, n0, names, a0, more):
                for t in range(PER_HALF):
                    n = n0 + PER_HALF * i + t
                    if t < PER_HALF - 1 or more:
                        split_lo(n + 1, (t + 1) % RAW, (t + 1) % SPLIT)
                    name = names[t // 4]
                    if name == "C" and t % 4 == 3:
                        for mt in range(MT):
                            groups_done(n, mt)
                            kt = bass.ds(4 * i + mt, 1)
                            own.mark(tt(z_p[:, kt, CW - 1:CW - 1 + TP].rearrange("p a n -> p (a n)"),
                                        bank[mt][:, 0:TP], u_t[:, mt, 0:TP], ALU.mult))
                            tt(z_s[:, kt, :, CW - 1:CW - 1 + ST].rearrange("p a s t -> p (a s) t"),
                               bank[mt][:, TP:NT].rearrange("p (s t) -> p s t", s=SB),
                               u_t[:, mt, TP:NT].rearrange("p (s t) -> p s t", s=SB), ALU.mult).then_inc(bank_turn, 1)
                    if name == "B":
                        mt = t % 4
                        if mt == 0:
                            dve.wait_ge(bank_turn, BT + MT * (G_UCB + 3 * i + 3))
                            own.wait()
                        kt = bass.ds(4 * i + mt, 1)

                        def wc(tap):
                            return vecT[:, bass.ds(4 * KT + tap * KC + 4 * i + mt, 1)]
                        c_p = conv[:, mt, 0:TP]
                        c_s = conv[:, mt, TP:NT].rearrange("p (s t) -> p s t", s=SB)

                        def z_at(tap):
                            return (z_p[:, kt, tap:tap + TP].rearrange("p a n -> p (a n)"),
                                    z_s[:, kt, :, tap:tap + ST].rearrange("p a s t -> p (a s) t"))
                        zp0, zs0 = z_at(0)
                        own.mark(ts(c_p, zp0, wc(0), None, ALU.mult))
                        own.mark(ts(c_s, zs0, wc(0), None, ALU.mult))
                        for tap in (1, 2):
                            zp, zs = z_at(tap)
                            own.wait()
                            own.mark(stt(c_p, zp, wc(tap), c_p, ALU.mult, ALU.add))
                            own.mark(stt(c_s, zs, wc(tap), c_s, ALU.mult, ALU.add))
                        if mt == 3:
                            own.wait()
                            for m in range(MT):
                                groups_done(n, m)
                                tt(yT[:, bass.ds(4 * i + m, 1), :].rearrange("p a n -> p (a n)"), bank[m][:, 0:NT],
                                   conv[:, m, :], ALU.mult).then_inc(bank_turn, 1)
                    if t % 3 == 2:
                        add_ada(a0 + ADA_PER_HALF * i + t // 3)

            split_lo(0, 0, 0)
            with own.loop(HALVES, MT + 6 * MT) as i:
                half_body(i, N_UCB, "uCB", ADA_FIRST, True)
            own.wait()
            own.mark(nc.vector.tensor_copy(z_end[:, :, 0:2], z_p[:, :, TP:TP + 2]))
            nc.vector.tensor_copy(z_end[:, :, 2:2 + 2 * SB].rearrange("p k (s t) -> p k s t", s=SB),
                                  z_s[:, :, :, ST:ST + 2]).then_inc(z_ready, 1)
            for i in range(HALVES):
                if i == 0:
                    dve.wait_ge(z_ps, 1)
                    own.mark(nc.vector.tensor_copy(z_rows[:, 0:512], bank[6][0:2 + 2 * SB, :]))
                    nc.vector.tensor_copy(z_rows[:, 512:DC], bank[7][0:2 + 2 * SB, :]).then_inc(z_out, 1)
                half_body(i, N_QKV, "qkv", ADA_FIRST + 2 * ADA_PER_HALF, i < HALVES - 1)

            dve.wait_ge(ada_mods, ADA_G + 1)
            add_bias(2 * KT, NMOD * KT)
            scaled(modG, KT, 2, 0.0)
            scaled(modA, 2 * KT, 4, 1.0)
            dve.wait_ge(lfr_ps, 1)
            for b in range(3):
                rows = min(P, NT - b * P)
                ins = nc.vector.tensor_copy(lfr[0:rows, b, :], bank[6][0:rows, H * b:H * b + H])
            ins.then_inc(lfr_done, 1)
            dve.wait_ge(cum_ps, 1)
            dve.wait_ge(fixed, 1)
            dve.wait_ge(s_zout, 32)
            for j in range(2):
                own.mark(ts(k_st[j][64:64 + H, :], bank[7][64:64 + H, 0:TP], -1.0, None, ALU.mult))
            own.mark(nc.vector.tensor_copy(cum_q[96:96 + H, :], bank[7][96:96 + H, 0:TP]))
            lfs = lf[:, TP:NT].rearrange("p (s t) -> p s t", s=SB)
            cqs = cq[0:H, :].rearrange("p (s t) -> p s t", s=SB)
            own.mark(nc.vector.tensor_copy(cqs[:, :, 0:1], lfs[:, :, 0:1]))
            for t in range(1, ST):
                own.wait()
                own.mark(tt(cqs[:, :, t:t + 1], cqs[:, :, t - 1:t], lfs[:, :, t:t + 1], ALU.add))
            own.wait()
            own.mark(nc.vector.tensor_copy(cq[32:32 + H, :], cq[0:H, :]))
            for s in range(SB):
                ins = ts(cumk[0:H, s, PAST:PAST + TS], cq[0:H, :], -1.0, None, ALU.mult)
            ins.then_inc(cum_done, 1)
            dve.wait_ge(suf_ps, 1)
            nc.vector.tensor_copy(suf[:, :, :, :], bank[6][:, 0:SB * NPG * H].rearrange(
                "p (s g h) -> p s g h", s=SB, g=NPG)).then_inc(suf_done, 1)

            def copy_k(pair, j):
                h = 2 * pair + j
                nc.vector.tensor_copy(k_st[j][0:DH, :], kT[DH * j:DH * j + DH, bass.ds(pair, 1), 0:TP].rearrange(
                    "p a n -> p (a n)")).then_inc(k_ready, 1)

            def max_head(h, j):
                dve.wait_ge(S_ps, h + 1)
                own.step()
                own.mark(nc.vector.tensor_tensor_reduce(
                    s_p[j][:, 0:P], bank[j][:, 0:P], mask_q[:, P:TP], 1.0, MASKED, ALU.add, ALU.max,
                    small[:, 4 * j:4 * j + 1]))
                own.mark(nc.vector.tensor_tensor_reduce(
                    s_p[j][:, P:3 * P], bank[j][:, P:3 * P], mask_q[:, :], 1.0, MASKED, ALU.add, ALU.max,
                    small[:, 4 * j + 1:4 * j + 2]))
                own.wait()
                ts(small[:, 4 * j:4 * j + 2], small[:, 4 * j:4 * j + 2], -1.0, None, ALU.mult).then_inc(S_max, 1)

            def norm_head(h, j):
                dve.wait_ge(S_exp, h + 1)
                own.mark(nc.vector.reciprocal(small[:, 4 * j + 2:4 * j + 4], small[:, 4 * j + 2:4 * j + 4]))
                own.wait()
                own.mark(ts(s_p[j][:, 0:P], s_p[j][:, 0:P], small[:, 4 * j + 2:4 * j + 3], None, ALU.mult))
                ts(s_p[j][:, P:3 * P], s_p[j][:, P:3 * P], small[:, 4 * j + 3:4 * j + 4], None,
                   ALU.mult).then_inc(S_norm, 1)

            with own.loop(PAGE_TURNS, 2 * (2 * 3 + 5 + 2 * 2 + 2)) as i:
                for j in range(2):
                    s = 2 * i + j
                    copy_k(s, 0)
                    copy_k(s, 1)
                    for n in (1, 3):
                        dve.wait_ge(sK_ps, 4 * s + n + 1)
                        if n == 1:
                            dve.wait_ge(sS_ps, 2 * s + 1)
                        nc.vector.tensor_copy(KTs[:, 4:8, (n // 2) * P:(n // 2) * P + P],
                                              bank[5][:, :].rearrange("p (f n) -> p f n", f=4)).then_inc(sK_d, 1)
                    max_head(2 * s, 0)
                    dve.wait_ge(sS_ps, 2 * s + 3)
                    for hf in range(2):
                        msk = mask_s[:, bass.ds(TS * s, TS)]
                        own.mark(nc.vector.tensor_copy(s_s[:, hf, 0:PAST], bank[6 + hf][:, 0:PAST]))
                        own.mark(tt(s_s[:, hf, PAST:PAST + TS], bank[6 + hf][:, PAST:PAST + TS], msk, ALU.add))
                    own.wait()
                    own.mark(nc.vector.tensor_reduce(small[:, 8:10], s_s[:, :, :], AX.X, ALU.max))
                    own.wait()
                    ts(small[:, 8:10], small[:, 8:10], -1.0, None, ALU.mult).then_inc(sS_max, 1)
                    max_head(2 * s + 1, 1)
                    norm_head(2 * s, 0)
                    dve.wait_ge(sS_exp, s + 1)
                    own.mark(nc.vector.reciprocal(small[:, 10:12], small[:, 10:12]))
                    own.wait()
                    own.mark(ts(s_s[:, 0, :], s_s[:, 0, :], small[:, 10:11], None, ALU.mult))
                    ts(s_s[:, 1, :], s_s[:, 1, :], small[:, 11:12], None, ALU.mult).then_inc(sS_norm, 1)
                    norm_head(2 * s + 1, 1)
                    dve.wait_ge(O_hi, s + 1)
                    at_ = bass.ds(s, 1)
                    tt(o_lo[:, at_, 0:TP].rearrange("p a n -> p (a n)"), bank[3][:, 0:TP],
                       o_hi[:, at_, 0:TP].rearrange("p a n -> p (a n)").bitcast(F32), ALU.subtract).then_inc(O_lo, 1)
                    dve.wait_ge(sO_hi, s + 1)
                    tok = bass.ds(TP + ST * s, ST)
                    for e in range(2):
                        src = bank[7][DH * e:DH * e + DH, 0:2 * P].rearrange("p (k c) -> p k c", c=32)
                        ins = tt(o_lo[DH * e:DH * e + DH, :, tok], src[:, :, ST * e:ST * e + ST],
                                 o_hi[DH * e:DH * e + DH, :, tok].bitcast(F32), ALU.subtract)
                    ins.then_inc(sO_lo, 1)

            dve.wait_ge(s_out, 16 * 5)
            split_lo(N_MIX, 0, 0)
            for c in range(2):
                split_act_lo(4 + c, yT, SK * c, y_hi, y_lo, SK * c)
            with own.loop(MIXES, MT) as i:
                for t in range(PER_MIX):
                    n = N_MIX + PER_MIX * i + t
                    split_lo(n + 1, (t + 1) % RAW, (t + 1) % SPLIT)
                    if t == 5:
                        for mt in range(MT):
                            groups_done(n, mt)
                            tt(m_T[:, bass.ds(MT * i + mt, 1), :].rearrange("p a n -> p (a n)"), bank[mt][:, 0:NT],
                               gate_a[:, mt, :], ALU.mult).then_inc(bank_turn, 1)
                    if t == 11:
                        for mt in range(MT):
                            groups_done(n, mt)
                            own.mark(tt(gate_b[:, mt, :], bank[mt][:, 0:NT], gate_b[:, mt, :], ALU.mult))
                            own.wait()
                            m = m_T[:, bass.ds(MT * i + mt, 1), :].rearrange("p a n -> p (a n)")
                            tt(m, m, gate_b[:, mt, :], ALU.add).then_inc(bank_turn, 1)
            for c in range(4):
                split_act_lo(6 + c, m_T, SK * c, a_hi, a_lo, SK * c)
            with dve.Fori(0, MIXES) as i:
                for t in range(PER_O):
                    split_lo(N_O + PER_O * i + t + 1, (t + 1) % RAW, (t + 1) % SPLIT)

            def add_scaled(c):
                own.wait()
                k0 = SK * c
                for kt in range(k0, k0 + SK):
                    own.mark(stt(xT[:, kt, 0:TP], r_src[0][:, kt, 0:TP], modG[:, kt, 0:1], xT[:, kt, 0:TP],
                                 ALU.mult, ALU.add))
                rs = seqs(r_src[0][:, k0:k0 + SK, TP:NT], SK)
                xs = seqs(xT[:, k0:k0 + SK, TP:NT], SK)
                own.mark(tt(rs, rs, cond(modG, k0, SK), ALU.mult))
                own.wait()
                return tt(xs, xs, rs, ALU.add)

            for c in range(4):
                sum_of_four(4 + c)
            mean_square(8)
            refine_root(2)
            r_src = [r_T]
            for c in range(4):
                times_rstd(r_T, r_T, c)
                add_scaled(c).then_inc(x1_done, 1)
            for c in range(4):
                sum_of_four(8 + c)
            mean_square(12)
            refine_root(3)
            for c in range(4):
                times_rstd(r_T, xT, c)
                modulate(r_T, modA, 3 * KT, c).then_inc(f_done, 1)
                split_act_lo(10 + c, r_T, SK * c, a_hi, a_lo, SK * c)
            scaled(modG, 3 * KT, 5, 0.0)
            with dve.Fori(0, F1S) as i:
                for t in range(PER_F1):
                    n = N_F1 + PER_F1 * i + t
                    split_lo(n + 1, (t + 1) % RAW, (t + 1) % SPLIT)
                    if t == 3:
                        for mt in range(MT):
                            dve.wait_ge(gate_done, MT * i + mt + 1)
                            tt(sg[:, mt, :], bank[mt][:, 0:NT], sg[:, mt, :], ALU.mult).then_inc(bank_turn, 1)
                    if t == 7:
                        for mt in range(MT):
                            groups_done(n, mt)
                            tt(hid[:, bass.ds(MT * i + mt, 1), :].rearrange("p a n -> p (a n)"),
                               bank[mt][:, 0:NT], sg[:, mt, :], ALU.mult).then_inc(bank_turn, 1)
            k = KF // SK
            for c in range(2):
                split_act_lo(14 + c, hid, SK * c, a_hi, a_lo, SK * c)
            for i in range(2):
                for t in range(PER_F2):
                    if t < PER_F2 - 1:
                        split_lo(N_F2 + PER_F2 * i + t + 1, (t + 1) % RAW, (t + 1) % SPLIT)
                    elif i == 0:
                        split_lo(N_F2 + PER_F2 * i + t + 1, 0, 0)
                    if t < PER_F2 - 2 or i == 0:
                        t2 = (t + 2) % PER_F2
                        split_act_lo(14 + PER_F2 * i + t + 2, hid, SK * (t2 % k), a_hi, a_lo, SK * (t2 % 4))
            for c in range(4):
                sum_of_four(12 + c)
            mean_square(16)
            refine_root(4)
            r_src[0] = f_T
            for c in range(4):
                times_rstd(f_T, f_T, c)
                add_scaled(c).then_inc(x_upd, 1)

        @block.gpsimd
        def _(pool):
            own = Own(pool, own_pool)
            g = nc.gpsimd
            own.mark(g.memset(ident[:, :], 0.0))
            own.mark(g.memset(m4_T[:, :], 0.0))
            own.mark(g.memset(ones[:, :], 1.0))
            own.mark(g.memset(mask_q[:, :], 0.0))
            own.mark(g.memset(sel[:, :, :], 0.0))
            own.mark(g.memset(selq[:, :, :], 0.0))
            own.wait()
            own.mark(g.affine_select(out=ident[:, :], in_=ident[:, :], compare_op=ALU.not_equal, fill=1.0, base=0,
                                     pattern=[[-1, P]], channel_multiplier=1))
            g.affine_select(out=m4_T[:, :].rearrange("j (r t) -> j r t", t=ST),
                            in_=m4_T[:, :].rearrange("j (r t) -> j r t", t=ST), compare_op=ALU.is_ge, fill=MASKED,
                            base=0, pattern=[[0, P // ST], [1, ST]], channel_multiplier=-1).then_inc(consts, 1)
            g.affine_select(out=mask_q[:, P:TP], in_=mask_q[:, P:TP], compare_op=ALU.is_ge, fill=MASKED, base=0,
                            pattern=[[-1, P]], channel_multiplier=1).then_inc(consts, 1)
            for par in range(2):
                part = sel[0:H, :, ST * par:ST * par + ST]
                ins = g.affine_select(out=part, in_=part, compare_op=ALU.not_equal, fill=1.0, base=-par,
                                      pattern=[[-2, KA], [0, ST]], channel_multiplier=1)
            ins.then_inc(consts, 1)
            pool.wait_ge(z_out, 1)
            pool.dma_start(conv_prompt[0, 0, :, :], z_rows[0:2, :]).then_inc(s_zout, 16)
            pool.dma_start(conv_sample[0].rearrange("s t n -> (s t) n"), z_rows[2:2 + 2 * SB, :]).then_inc(s_zout, 16)
            pool.wait_ge(ada_turn, RAW + SK * ADA_G)
            pool.wait_ge(s_table, 16)
            pages = lfc[:, :, :, :].rearrange("p s g h -> p (s g) h")
            with pool.Fori(0, SB * NPG) as n:
                r = pool.value_load(table[0:1, bass.ds(n, 1)], min_val=0, max_val=POOL - 1)
                pool.dma_start(pages[:, bass.ds(n, 1), :].rearrange("p a h -> p (a h)"),
                               cache_logf[0, bass.ds(r, 1), :, :].rearrange("a p h -> p (a h)")).then_inc(s_lfc, 16)
            own.mark(g.memset(cumk[:, :, :], 0.0))
            own.mark(g.memset(q_bd[:, :, :], 0.0))
            for j in range(2):
                own.wait()
                own.mark(g.memset(q_st[j][64:112, :], 0.0))
                own.wait()
                own.mark(g.memset(k_st[j][64:112, :], 0.0))
            own.wait()
            own.mark(g.memset(cumk[32:48, :, :], 1.0))
            own.wait()
            own.mark(g.memset(k_st[0][96:112, :], 1.0))
            own.wait()
            g.memset(k_st[1][96:112, :], 1.0).then_inc(fixed, 1)
            pool.wait_ge(fixed, 1)
            pool.wait_ge(mm_turn, MT * (SPLIT + N_MIX))
            own.mark(g.memset(upto[:, :], 1.0))
            own.mark(g.memset(after[:, :], 1.0))
            own.wait()
            g.affine_select(out=upto[:, 0:P], in_=upto[:, 0:P], compare_op=ALU.is_ge, fill=0.0, base=0,
                            pattern=[[1, P]], channel_multiplier=-1)
            g.affine_select(out=after[:, :], in_=after[:, :], compare_op=ALU.is_gt, fill=0.0, base=0,
                            pattern=[[-1, P]], channel_multiplier=1).then_inc(sums_ready, 1)
            pool.wait_ge(lfr_done, 1)
            for b in range(2):
                pool.dma_start(logf_prompt[0, 0, b * P:b * P + P, :], lfr[:, b, :]).then_inc(s_out, 16)
            pool.dma_start(logf_sample[0].rearrange("s t h -> (s t) h"), lfr[0:TS, 2, :]).then_inc(s_out, 16)
            pool.wait_ge(rowT_out, 6)
            pool.dma_start(k_prompt[0, 0].rearrange("(b p) h d -> p b (h d)", p=P), k_rows[:, 0:2, :]).then_inc(s_kout, 16)
            pool.dma_start(k_sample[0].rearrange("s t h d -> (s t) (h d)"), k_rows[0:TS, 2, :]).then_inc(s_kout, 16)
            pool.wait_ge(rowT_out, 12)
            pool.dma_start(v_prompt[0, 0].rearrange("(b p) h d -> p b (h d)", p=P), v_rows[:, 0:2, :]).then_inc(s_out, 16)
            pool.dma_start(v_sample[0].rearrange("s t h d -> (s t) (h d)"), v_rows[0:TS, 2, :]).then_inc(s_out, 16)
            pool.wait_ge(pool_sel, 1)
            pool.wait_ge(cum_done, 1)
            pool.wait_ge(sufT_done, 1)

            def extra_rows(h, j):
                pool.wait_ge(S_max, h + 1)
                for p0, src in ((64, ones), (96, cum_q)):
                    rows = slice(p0, p0 + H)
                    pick = ident[rows, bass.ds(p0 + h, 1)].broadcast_to([H, TP])
                    own.wait()
                    ins = g.tensor_tensor(q_st[j][rows, :], src[rows, 0:TP], pick, ALU.mult)
                    if p0 == 64:
                        own.mark(ins)
                ins.then_inc(qe_ready, 1)
                pool.wait_ge(qe_ready, h + 1)

            with own.loop(SB, 3) as s:
                extra_rows(2 * s, 0)
                extra_rows(2 * s + 1, 1)
                pool.wait_ge(sS_ps, 2 * s + 1)
                own.mark(g.tensor_copy(cumk_s[:, :], cumk[:, bass.ds(s, 1), :].rearrange("p a n -> p (a n)")))
                own.wait()
                both = [KA, 2, ST]
                g.tensor_tensor(selq[32:32 + H, :, 0:2 * ST].rearrange("p k (e t) -> p k e t", e=2),
                                sel[32:32 + H, :, :].rearrange("p k (e t) -> p k e t", e=2),
                                cq[32:32 + H, bass.ds(ST * s, ST)].unsqueeze(1).unsqueeze(1).broadcast_to([H] + both),
                                ALU.mult).then_inc(sSel, 1)
                pool.wait_ge(O_ps, 2 * s + 1)
                pool.wait_ge(sSel, s + 1)
                g.tensor_copy(v_st[:, :, :], v_rows[:, 0:2, bass.ds(P * s, P)]).then_inc(v_ready, 1)
                pool.wait_ge(v_ready, s + 1)
            for c in range(4):
                pool.wait_ge(y_out, 3 * c + 3)
                cols = slice(SN * c, SN * c + SN)
                pool.dma_start(y_prompt[0].rearrange("(b p) n -> p b n", p=P)[:, :, cols], y_rows[:, 0:2, cols]).then_inc(s_out, 16)
                pool.dma_start(y_sample.rearrange("s t n -> (s t) n")[:, cols], y_rows[0:TS, 2, cols]).then_inc(s_out, 16)
            pool.wait_ge(s_out, 16 * (5 + 8))
            pool.wait_ge(s_kout, 32)
            pool.wait_ge(s_zout, 32)


_INS = ["x_prompt", "x_sample", "cache_k", "cache_v", "cache_logf", "state_conv", "page_table", "c_prompt",
        "c_sample", "w_ada", "b_ada", "g_pre1", "w_in", "b_f", "w_conv", "w_oa", "w_ob", "w_o", "g_post1",
        "g_pre2", "w_ffn_in", "w_ffn_out", "g_post2"]


def kernel(**inputs):
    from concourse import bacc
    from concourse.bass_utils import run_bass_kernel_spmd

    nc = bacc.Bacc("TRN2", target_bir_lowering=False, num_devices=1)
    arrays, args = {}, []
    for name in _INS:
        a = np.ascontiguousarray(inputs[name])
        arrays[f"in_{name}"] = a
        args.append(nc.dram_tensor(f"in_{name}", a.shape, mybir.dt.from_np(a.dtype), kind="ExternalInput").ap())
    B, T, D = arrays["in_x_prompt"].shape
    SB, ST, _ = arrays["in_x_sample"].shape
    L, _, _, H, DH = arrays["in_cache_k"].shape
    _, _, CP, DC = arrays["in_state_conv"].shape
    outs = [(B, T, D), (SB, ST, D), (L, B, T, H, DH), (L, B, T, H, DH), (L, B, T, H), (L, B, CP, DC),
            (L, SB, ST, H, DH), (L, SB, ST, H, DH), (L, SB, ST, H), (L, SB, CP, DC)]
    for i, shape in enumerate(outs):
        args.append(nc.dram_tensor(f"out_{i}", shape, F32, kind="ExternalOutput").ap())
    layer(nc, *args)
    r = run_bass_kernel_spmd(nc, [arrays], core_ids=[0])
    return tuple(r.results[0][f"out_{i}"] for i in range(len(outs)))
```

```python
from contextlib import ExitStack, contextmanager

import numpy as np

import concourse.bass as bass
import concourse.mybir as mybir
from concourse.alu_op_type import AluOpType as ALU

F32 = mybir.dt.float32
F32R = mybir.dt.float32r
I32 = mybir.dt.int32
ACT = mybir.ActivationFunctionType
AX = mybir.AxisListType

P = 128
EPS = 1e-6
MASKED = -1e30
RAW = 4
SPLIT = 2
SK = 4
SN = 512
MT = SN // P


class Own:

    def __init__(self, eng, sem):
        self.eng, self.sem, self.n, self.turn = eng, sem, 0, 0

    def mark(self, ins):
        ins.then_inc(self.sem, 1)
        self.n += 1

    def step(self):
        self.eng.sem_inc(self.sem, 1)
        self.n += 1

    def wait(self):
        self.eng.wait_ge(self.sem, self.n + self.turn)

    @contextmanager
    def loop(self, count, per):
        start = self.n
        with self.eng.Fori(0, count) as i:
            self.turn = i * per
            yield i
            assert self.n - start == per, (self.n - start, per)
        self.turn = 0
        self.n = start + per * count


def layer(nc, x_prompt, x_sample, cache_k, cache_v, cache_logf, state_conv, page_table, c_prompt,
          c_sample, w_ada, b_ada, g_pre1, w_in, b_f, w_conv, w_oa, w_ob, w_o, g_post1, g_pre2,
          w_ffn_in, w_ffn_out, g_post2, y_prompt, y_sample, k_prompt, v_prompt, logf_prompt,
          conv_prompt, k_sample, v_sample, logf_sample, conv_sample):
    _, TP, D = x_prompt.shape
    SB, ST, _ = x_sample.shape
    TS = SB * ST
    NT = TP + TS
    _, POOL, PAGE, H, DH = cache_k.shape
    NPG = page_table.shape[1]
    DA = H * DH
    DC = w_conv.shape[2]
    CW = w_conv.shape[1]
    DFF = w_ffn_out.shape[1]
    KT = D // P
    KA = DA // P
    KC = DC // P
    KF = DFF // P
    NC = 1 + SB
    NMOD = 6
    SCALE = DH ** -0.5
    PAST = NPG * PAGE
    assert PAGE == P and NPG == 2 and DH == 64 and TP == 2 * P and CW == 3 and KT == 16
    assert KA == 8 and KC == 8 and NT <= 512 and KF == 11 * SK and SB == 8 and ST == 4
    CQ, CK, CV = 0, DA, 2 * DA
    CF = 3 * DA
    CU = CF + H
    CB, CC = CU + DC, CU + 2 * DC
    CGA = CU + 3 * DC
    CGB = CGA + D

    HALVES = DC // SN
    PER_HALF = 3 * KT // SK
    N_UCB = 0
    N_QKV = N_UCB + HALVES * PER_HALF
    N_MIX = N_QKV + HALVES * PER_HALF
    MIXES = D // SN
    PER_MIX = 2 * (KT // SK) + 2 * (KA // SK)
    N_O = N_MIX + MIXES * PER_MIX
    PER_O = KT // SK
    N_F1 = N_O + MIXES * PER_O
    F1S = DFF // SN
    PER_F1 = 2 * KT // SK
    N_F2 = N_F1 + F1S * PER_F1
    PER_F2 = 2 * (KF // SK)
    G_UCB = 0
    G_QKV = G_UCB + 3 * HALVES
    G_MIX = G_QKV + 3 * HALVES
    G_O = G_MIX + 4 * MIXES
    G_F1 = G_O + MIXES
    G_F2 = G_F1 + 2 * F1S
    G_END = G_F2 + MIXES
    BT = KT - MT
    R_PAGES = N_MIX // RAW
    PAGE_TURNS = SB // 2
    R_MIX = R_PAGES + NPG * PAGE_TURNS
    R_O = R_MIX + MIXES * PER_MIX // RAW
    R_F1 = R_O + MIXES * PER_O // RAW
    R_F2 = R_F1 + F1S * PER_F1 // RAW
    ADA_G = NMOD * D // SN
    ADA_FIRST = 2 * D // SN
    ADA_PER_HALF = PER_HALF // SK
    ADA_MAIN = ADA_FIRST + 2 * HALVES * ADA_PER_HALF
    assert ADA_G == ADA_MAIN + MIXES

    ctx = ExitStack()
    with ctx:
        def sem(name):
            return ctx.enter_context(nc.semaphore(name))

        base = -(-nc.sbuf_base // 64) * 64
        at = [base]

        def place(name, shape, dt=F32, where=None):
            size = 4 * int(np.prod(shape[1:]))
            if where is None:
                where = at[0]
                at[0] += -(-size // 32) * 32
            assert where % 32 == 0, name
            return nc.alloc_sbuf_tensor_at(name, shape, dt, offset=where)

        ident = place("ident", [P, P])
        ones = place("ones", [P, TP])
        mask_q = place("mask_q", [P, TP])
        assert SB * (TS + ST) == NT
        sqr = place("sqr", [P, NT], where=at[0])
        mask_s = place("mask_s", [P, SB * (TS + ST)])
        vecT = place("vecT", [P, 4 * KT + CW * KC])
        bT = place("bT", [P, NMOD * KT])
        mods = place("mods", [P, NMOD * KT, NC])
        modA = place("modA", [P, KT, NC])
        modG = place("modG", [P, KT, NC])
        cT = place("cT", [P, KT, 32])
        sel = place("sel", [48, KA, 2 * ST])
        selq = place("selq", [48, KA, 32])
        cq = place("cq", [P, TS])
        lf = place("lf", [H, NT])
        lfr = place("lfr", [P, 3, H])
        bf = place("bf", [H, 1])
        small = place("small", [P, 16])
        table = place("table", [1, SB * NPG], I32)
        ada_sb = place("ada_sb", [P, SN])
        rstd = place("rstd", [P, NT])
        lfc = place("lfc", [P, SB, NPG, H], where=at[0] - -(-4 * NT // 32) * 32)
        cum_q = place("cum_q", [P, TP], where=at[0] - -(-4 * NT // 32) * 32)

        raw = [place(f"raw{s}", [P, SK, SN]) for s in range(RAW)]
        off_split = at[0]
        w_hi, w_lo = zip(*[(place(f"w_hi{s}", [P, SK, SN], F32R), place(f"w_lo{s}", [P, SK, SN], F32R))
                           for s in range(SPLIT)])
        xT = place("xT", [P, KT, NT])
        off_act = at[0]
        a_hi = place("a_hi", [P, KT, NT], F32R)
        a_lo = place("a_lo", [P, KT, NT], F32R)
        R = at[0]
        top = nc.sbuf_usable_end
        assert R + RAW * SK * SN * 4 + 4 * KA * NT * 4 + 4672 <= top
        B_ACT8 = KA * NT * 4
        ada = [place(f"ada{s}", [P, SK, SN], where=R + s * SK * SN * 4) for s in range(RAW)]
        o_qkv = R + RAW * SK * SN * 4
        qT = place("qT", [P, KA, NT], where=o_qkv)
        kT = place("kT", [P, KA, NT], where=o_qkv + B_ACT8)
        vT = place("vT", [P, KA, NT], where=o_qkv + 2 * B_ACT8)
        yT = place("yT", [P, KC, NT], where=o_qkv + 3 * B_ACT8)
        tail = o_qkv + 4 * B_ACT8
        sq4 = place("sq4", [P, SK, NT], where=tail)
        x_rows = place("x_rows", [P, 3, D], where=off_split)
        c_rows = place("c_rows", [NC, D], where=off_split + 3 * D * 4)
        c_sig = place("c_sig", [NC, D], where=off_act)
        vec_rows = place("vec_rows", [4 * KT + CW * KC, P], where=off_act + D * 4)
        b_rows = place("b_rows", [NMOD * KT, P], where=off_act + D * 4 + 512)
        st_rows = place("st_rows", [SB * 2, DC], where=off_act + D * 4 + 1024)
        xn = place("xn", [P, KT, NT], where=o_qkv)
        o = o_qkv
        z_p = place("z_p", [P, KC, CW - 1 + TP], where=o); o += KC * (CW - 1 + TP) * 4
        z_s = place("z_s", [P, KC, SB, CW - 1 + ST], where=o); o += KC * SB * (CW - 1 + ST) * 4
        u_t = place("u_t", [P, MT, NT], where=o); o += MT * NT * 4
        conv = place("conv", [P, MT, NT], where=o); o += MT * NT * 4
        o = o_qkv + 20480
        lfz = place("lfz", [H, NT], where=o); o += NT * 4
        lfe = place("lfe", [H, NT], where=o); o += NT * 4
        st_T = place("st_T", [P, KC, SB, 2], where=o); o += KC * SB * 2 * 4
        m4_T = place("m4_T", [ST, P], where=o); o += P * 4
        wf = place("wf", [P, KT, H], where=o); o += KT * H * 4
        wf_hi = place("wf_hi", [P, KT, H], F32R, where=o); o += KT * H * 4
        wf_lo = place("wf_lo", [P, KT, H], F32R, where=o); o += KT * H * 4
        assert o <= o_qkv + 3 * B_ACT8
        z_end = place("z_end", [P, KC, 2 + 2 * SB], where=tail)
        z_rows = place("z_rows", [2 + 2 * SB, DC], where=tail + 576)
        assert tail + 576 + DC * 4 <= top
        o_hi = place("o_hi", [P, KA, NT], F32R, where=R)
        o_lo = place("o_lo", [P, KA, NT], F32R, where=R + B_ACT8)
        k_rows = place("k_rows", [P, 3, DA], where=R)
        upto = place("upto", [P, TP], where=R + 3 * DA * 4)
        after = place("after", [P, P], where=R + 3 * DA * 4 + TP * 4)
        suf = place("suf", [P, SB, NPG, H], where=R + 3 * DA * 4 + (TP + P) * 4)
        w = R + 2 * B_ACT8
        cumk = place("cumk", [48, SB, PAST + TS], where=w); w += SB * (PAST + TS) * 4
        q_st = [place(f"q_st{j}", [112, TP], where=w + j * TP * 4) for j in range(2)]; w += 2 * TP * 4
        q_bd = place("q_bd", [P, KA, 32], where=w); w += KA * 32 * 4
        k_st_at = w
        assert w <= o_qkv, (w, o_qkv)
        w = off_split
        KTs = [place(f"KTs{j}", [P, KA, PAST + TS], where=x) for j, x in ((0, w), (1, o_qkv + 2 * B_ACT8))]; w += KA * (PAST + TS) * 4
        v_rows = place("v_rows", [P, 2, DA], where=w); w += 2 * DA * 4
        w = max(w, off_split + 2 * SK * SN * 4)
        v_new = place("v_new", [P, DA], where=w); w += DA * 4
        pT_s = place("pT_s", [P, 2, 3 * P], where=w); w += 6 * P * 4
        pT_p = place("pT_p", [P, 3 * P], where=w); w += 3 * P * 4
        s_s = place("s_s", [P, 2, PAST + TS], where=w); w += 2 * (PAST + TS) * 4
        v_st = [place(f"v_st{j}", [P, 2, P], where=w + j * 2 * P * 4) for j in range(2)]; w += 4 * P * 4
        cumk_s = place("cumk_s", [48, PAST + TS], where=w); w += (PAST + TS) * 4
        assert w <= off_split + 2 * SPLIT * SK * SN * 4, w - off_split
        w = tail
        s_p = [place(f"s_p{j}", [P, 3 * P], where=w + j * 3 * P * 4) for j in range(2)]; w += 6 * P * 4
        o_s = place("o_s", [P, 2, P], where=w); w += 2 * P * 4
        k_st = [place(f"k_st{j}", [112, TP], where=k_st_at + j * TP * 4) for j in range(2)]
        assert k_st_at + 2 * TP * 4 <= o_qkv, (k_st_at + 2 * TP * 4, o_qkv)
        assert w <= top
        y_hi = place("y_hi", [P, KC, NT], F32R, where=o_qkv)
        y_lo = place("y_lo", [P, KC, NT], F32R, where=o_qkv + B_ACT8)
        m_T = place("m_T", [P, KT, NT], where=o_qkv + 2 * B_ACT8)
        gate_a = place("gate_a", [P, MT, NT], where=R + 2 * B_ACT8)
        gate_b = place("gate_b", [P, MT, NT], where=R + 2 * B_ACT8 + MT * NT * 4)
        r_T = place("r_T", [P, KT, NT], where=R)
        sq4b = place("sq4b", [P, SK, NT], where=R + KT * NT * 4)
        x1A = place("x1A", [P, KT, NT], where=R + (KT + SK) * NT * 4)
        ada_o = [place(f"ada_o{s}", [P, SK, SN], where=R + KT * NT * 4 + s * SK * SN * 4) for s in range(RAW)]
        assert R + KT * NT * 4 + RAW * SK * SN * 4 <= o_qkv + 2 * B_ACT8
        hid = place("hid", [P, KF, NT], where=R)
        f_T = place("f_T", [P, KT, NT], where=R + KF * NT * 4)
        assert KF * NT * 4 + KT * NT * 4 <= tail - R
        sg = place("sg", [P, MT, NT], where=tail)
        y_rows = place("y_rows", [P, 3, D], where=R)

        bank = [ctx.enter_context(nc.psum_tensor(f"bank{b}", [P, 512], F32)) for b in range(8)]

        s_c, s_rows, s_x, s_wf, s_table, s_lfc = (sem(n) for n in (
            "c_in", "rows_in", "x_in", "wf_in", "table_in", "lfc_in"))
        raw_full = [sem(f"raw_full{s}") for s in range(RAW)]
        ada_full = [sem(f"ada_full{s}") for s in range(RAW)]
        s_out, s_kout = sem("out_done"), sem("kout_done")
        raw_turn, mm_turn, ada_turn, bank_turn = (sem(n) for n in (
            "raw_turn", "mm_turn", "ada_turn", "bank_turn"))
        hi_done = sem("hi_done")
        act_hi, act_lo = sem("act_hi"), sem("act_lo")
        consts, c_sigm, c_silu, cT_ps, cT_ready = (sem(n) for n in (
            "consts", "c_sigm", "c_silu", "cT_ps", "cT_ready"))
        rows_ps, vec_ready, x_ps = sem("rows_ps"), sem("vec_ready"), sem("x_ps")
        ada_copied, ada_T, ada_mods = (sem(n) for n in ("ada_copied", "ada_T", "ada_mods"))
        sq_done, sqr_done, ms_ps, ms_done, root_done, x1_done, x1A_done, f_done = (sem(n) for n in (
            "sq_done", "sqr_done", "ms_ps", "ms_done", "root_done", "x1_done", "x1A_done", "f_done"))
        rstd_ready, normed = sem("rstd_ready"), sem("normed")
        x_upd = sem("x_upd")
        gate_done, m_done = sem("gate_done"), sem("m_done")
        f_ps, f_z, f_ln, f_lf, lfr_ps, lfr_done, cum_ps, cum_done = (sem(n) for n in (
            "f_ps", "f_z", "f_ln", "f_lf", "lfr_ps", "lfr_done", "cum_ps", "cum_done"))
        wf_hi_done, wf_split = sem("wf_hi_done"), sem("wf_split")
        s_zout, m4_ps, m4_done = sem("zout_done"), sem("m4_ps"), sem("m4_done")
        fixed, cleared, pool_sel, sums_ready = (sem(n) for n in ("fixed", "cleared", "pool_sel", "sums_ready"))
        z_ready, z_ps, z_out = sem("z_ready"), sem("z_ps"), sem("z_out")
        rowT_ps, rowT_a, rowT_d, suf_ps, suf_done, sufT_ps, sufT_done = (sem(n) for n in (
            "rowT_ps", "rowT_a", "rowT_d", "suf_ps", "suf_done", "sufT_ps", "sufT_done"))
        q_ready, k_ready, qe_ready, v_ready, S_ps, S_max, S_exp, S_norm, PT_ps, PT_out, O_ps, O_hi, O_lo = (
            sem(n) for n in ("q_ready", "k_ready", "qe_ready", "v_ready", "S_ps", "S_max", "S_exp",
                             "S_norm", "PT_ps", "PT_out", "O_ps", "O_hi", "O_lo"))
        sK_ps, sK_a, sK_d, sQ, sSel, sS_ps, sS_max, sS_exp, sS_norm, sP_ps, sP_out, sO_sb, sOT, sO_hi, sO_lo = (
            sem(n) for n in ("sK_ps", "sK_a", "sK_d", "sQ", "sSel", "sS_ps", "sS_max", "sS_exp", "sS_norm",
                             "sP_ps", "sP_out", "sO_sb", "sOT", "sO_hi", "sO_lo"))
        page_used = sem("page_used")
        y_ps, y_out = sem("y_ps"), sem("y_out")
        own_act, own_dve, own_pool, own_sp = sem("own_act"), sem("own_dve"), sem("own_pool"), sem("own_sp")

        def slots(w):
            return w[0].rearrange("(q a p) n -> q p a n", a=SK, p=P)

        wv_ada, wv_in, wv_oa, wv_ob, wv_o, wv_f1, wv_f2 = map(
            slots, (w_ada, w_in, w_oa, w_ob, w_o, w_ffn_in, w_ffn_out))
        half_cols = {"u": CU, "C": CC, "B": CB, "q": CQ, "k": CK, "v": CV}

        def copy_rows(eng, copy, sem_, first, end=12):
            for n in range(first, end, 2):
                b, half = n % 6 // 2, n % 2
                rows = min(P, NT - b * P)
                dst = k_rows[:, b, :] if n < 6 else v_rows[:, b, :] if b < 2 else v_new[:, :]
                eng.wait_ge(rowT_ps, n + 1)
                copy(dst[0:rows, half * 512:half * 512 + 512], bank[n % 4][0:rows, :]).then_inc(sem_, 1)

        block = ctx.enter_context(nc.Block())

        @block.sync
        def _(sp):
            def load_ada(m, s, src, ring=ada):
                sp.wait_ge(ada_turn, m + 1)
                sp.dma_start(ring[s][:, :, :], src).then_inc(ada_full[s], 16)

            def load_w(n, s, src):
                sp.wait_ge(raw_turn, n + 1)
                sp.dma_start(raw[s][:, :, :], src).then_inc(raw_full[s], 16)

            load_w(N_UCB, 0, wv_in[0, :, :, CU:CU + SN])
            with sp.Fori(0, ADA_FIRST // 2) as c:
                for e in range(2):
                    for q in range(SK):
                        load_ada(SK * (2 * c + e) + q, q, wv_ada[q, :, :, bass.ds(e * D + c * SN, SN)])
            def load_half(i, n0, names, a0, first=0):
                for t in range(PER_HALF):
                    if t >= first:
                        col = half_cols[names[t // 4]] + i * SN
                        load_w(n0 + PER_HALF * i + t, t % RAW, wv_in[t % 4, :, :, bass.ds(col, SN)])
                    if t % 4 < 2:
                        ga = a0 + ADA_PER_HALF * i + t // 4
                        for q in (2 * (t % 4), 2 * (t % 4) + 1):
                            load_ada(SK * ga + q, q, wv_ada[q, :, :, bass.ds(ga * SN, SN)])

            for i in range(HALVES):
                load_half(i, N_UCB, "uCB", ADA_FIRST, 1 - i)
            with sp.Fori(0, HALVES) as i:
                load_half(i, N_QKV, "qkv", ADA_FIRST + HALVES * ADA_PER_HALF)
            sp.wait_ge(s_table, 16)
            sp.wait_ge(raw_turn, RAW + N_MIX)
            with sp.Fori(0, PAGE_TURNS) as i:
                for j in range(2):
                    s = 2 * i + j
                    pages = [sp.value_load(table[0:1, bass.ds(s * NPG + pg, 1)], min_val=0, max_val=POOL - 1)
                             for pg in range(NPG)]
                    for slot, src in ((2 * j, cache_k), (2 * j + 1, cache_v)):
                        if src is cache_k:
                            sp.wait_ge(sK_ps, 4 * (s + 1))
                        else:
                            sp.wait_ge(page_used, s + 1)
                        for pg, r in enumerate(pages):
                            sp.dma_start(raw[slot][:, 2 * pg:2 * pg + 2, :].rearrange("p a n -> p (a n)"),
                                         src[0, bass.ds(r, 1), :, :, :].rearrange("a p h d -> p (a h d)")
                                         ).then_inc(raw_full[slot], 16)
            with sp.Fori(0, MIXES) as i:
                for t in range(PER_MIX):
                    if t in (0, 2):
                        sp.wait_ge(sK_ps, 2 * 4 + 4 * (SB - 1 + t // 2))
                    if t in (1, 3):
                        sp.wait_ge(page_used, 2 + SB - 1 + t // 2)
                    if t < 4:
                        src = wv_in[t, :, :, bass.ds(CGA + i * SN, SN)]
                    elif t < 6:
                        src = wv_oa[t - 4, :, :, bass.ds(i * SN, SN)]
                    elif t < 10:
                        src = wv_in[t - 6, :, :, bass.ds(CGB + i * SN, SN)]
                    else:
                        src = wv_ob[t - 10, :, :, bass.ds(i * SN, SN)]
                    if t in (4, 10):
                        sp.wait_ge(raw_turn, N_MIX + PER_MIX * i + t + 1)
                        sp.sem_inc(own_sp, 1)
                        sp.dma_start(raw[t % RAW][:, :, :], src).then_inc(raw_full[t % RAW], 16)
                    else:
                        load_w(N_MIX + PER_MIX * i + t, t % RAW, src)
            with sp.Fori(0, MIXES) as i:
                for t in range(PER_O):
                    load_w(N_O + PER_O * i + t, t, wv_o[t, :, :, bass.ds(i * SN, SN)])
                sp.wait_ge(mm_turn, MT * (SPLIT + N_O))
                sp.wait_ge(m_done, MIXES + 1)
                for q in range(SK):
                    ga = ADA_MAIN + i
                    load_ada(SK * ga + q, q, wv_ada[q, :, :, bass.ds(ga * SN, SN)], ada_o)
            with sp.Fori(0, F1S) as i:
                for t in range(PER_F1):
                    col = (t // 4) * DFF + i * SN
                    load_w(N_F1 + PER_F1 * i + t, t % RAW, wv_f1[t % 4, :, :, bass.ds(col, SN)])
            with sp.Fori(0, 2) as i:
                for t in range(PER_F2):
                    late = {0: 2, 1: 2}.get(t, 0)
                    sp.wait_ge(raw_turn, N_F2 + PER_F2 * i + t + 1 + late)
                    sp.dma_start(raw[t % RAW][:, :, :],
                                 wv_f2[t % (KF // SK), :, :, bass.ds((2 * i + t // (KF // SK)) * SN, SN)]
                                 ).then_inc(raw_full[t % RAW], 16)

        @block.tensor
        def _(pe):
            def product(n, first, last, G, kt0, hi, lo, buf):
                pe.wait_ge(raw_turn, RAW + n + 1)
                for mt in range(MT):
                    if first:
                        pe.wait_ge(bank_turn, BT + MT * G + mt + 1)
                    cols = slice(mt * P, mt * P + P)
                    for a in range(SK):
                        acc, kt = bank[mt][:, 0:NT], kt0 + a
                        pe.matmul(acc, w_hi[buf][:, a, cols], lo[:, kt, :], start=first and a == 0, stop=False)
                        pe.matmul(acc, w_hi[buf][:, a, cols], hi[:, kt, :], start=False, stop=False)
                        mm = pe.matmul(acc, w_lo[buf][:, a, cols], hi[:, kt, :], start=False,
                                       stop=last and a == SK - 1)
                    mm.then_inc(mm_turn, 1)

            def ada_slot(s, q, use, ring=ada):
                pe.wait_ge(ada_full[s], 16 * use)
                for a in range(SK):
                    mm = pe.matmul(bank[4][32 * a:32 * a + 32, :], cT[:, SK * q + a, :], ring[s][:, a, :],
                                   start=q == 0, stop=q == SK - 1, tile_position=(0, 32 * a))
                mm.then_inc(ada_turn, 1)

            def ada_transpose(g):
                pe.wait_ge(ada_copied, g + 2)
                pe.wait_ge(ada_mods, g + 1)
                for m in range(MT):
                    mm = pe.transpose(bank[5][:, m * P:m * P + P], ada_sb[:, m * P:m * P + P], ident[:, :])
                mm.then_inc(ada_T, 1)

            pe.sem_inc(mm_turn, MT * SPLIT)
            pe.sem_inc(ada_turn, RAW)
            pe.sem_inc(ada_T, 1)
            pe.sem_inc(page_used, 2)
            pe.sem_inc(sK_ps, 2 * 4)
            pe.sem_inc(sS_ps, 1)
            pe.sem_inc(O_ps, 1)
            pe.sem_inc(sOT, 1)
            pe.wait_ge(consts, 1)
            pe.wait_ge(c_silu, 1)
            for kt in range(KT):
                mm = pe.transpose(bank[6][:, NC * kt:NC * (kt + 1)], c_rows[:, kt * P:kt * P + P], ident[0:NC, 0:NC])
            mm.then_inc(cT_ps, 1)
            pe.transpose(bank[7][:, 0:ST], m4_T[:, :], ident[0:ST, 0:ST]).then_inc(m4_ps, 1)
            pe.wait_ge(s_rows, 16 * 8)
            nv, nb = 4 * KT + CW * KC, NMOD * KT
            pe.transpose(bank[4][:, 0:nv], vec_rows[:, :], ident[0:nv, 0:nv])
            pe.transpose(bank[4][:, P:P + nb], b_rows[:, :], ident[0:nb, 0:nb])
            for kt in range(KC):
                mm = pe.transpose(bank[5][:, 2 * SB * kt:2 * SB * (kt + 1)], st_rows[:, kt * P:kt * P + P],
                                  ident[0:2 * SB, 0:2 * SB])
            mm.then_inc(rows_ps, 1)

            def turn_x(kt):
                pe.wait_ge(s_x, 48)
                if kt >= 4:
                    pe.wait_ge(bank_turn, kt - 4 + 1)
                for b in range(3):
                    rows = min(P, NT - b * P)
                    mm = pe.transpose(bank[kt % 4][:, b * P:b * P + rows], x_rows[0:rows, b, kt * P:kt * P + P],
                                      ident[0:rows, 0:rows])
                mm.then_inc(x_ps, 1)

            def sum_squares(c, n, sq):
                pe.wait_ge(sq_done, n + 1)
                for a in range(SK):
                    mm = pe.matmul(bank[7][:, 0:NT], ones[:, 0:P], sq[:, a, :], start=c == 0 and a == 0,
                                   stop=c == 3 and a == SK - 1)
                mm.then_inc(ms_ps, 1)

            pe.wait_ge(cT_ready, 1)
            pe.wait_ge(vec_ready, 1)
            pe.wait_ge(m4_done, 1)
            pe.wait_ge(consts, 2)
            for g in range(ADA_FIRST):
                pe.wait_ge(ada_copied, g + 1)
                for q in range(SK):
                    ada_slot(q, q, g + 1)
                if g < 2:
                    for kt in range(KT // 2 * g, KT // 2 * (g + 1)):
                        turn_x(kt)
                if 1 <= g <= 4:
                    sum_squares(g - 1, g - 1, sq4)
                ada_transpose(g)
            def ada_beside(g, t, ring):
                if t < 2:
                    if t == 0:
                        pe.wait_ge(ada_copied, g + 1)
                    for q in (2 * t, 2 * t + 1):
                        ada_slot(q, q, g + 1, ring)
                if t == 3:
                    ada_transpose(g)

            for n0, g0, a0, names in ((N_UCB, G_UCB, ADA_FIRST, "uCB"),
                                      (N_QKV, G_QKV, ADA_FIRST + HALVES * ADA_PER_HALF, "qkv")):
                with pe.Fori(0, HALVES) as i:
                    for t in range(PER_HALF):
                        pe.wait_ge(act_lo, t % 4 + 1)
                        product(n0 + PER_HALF * i + t, t % 4 == 0, t % 4 == 3, g0 + 3 * i + t // 4,
                                SK * (t % 4), a_hi, a_lo, t % SPLIT)
                        ada_beside(a0 + ADA_PER_HALF * i + t // 4, t % 4, ada)
                if names == "uCB":
                    pe.wait_ge(wf_split, 1)
                    acc = bank[6][0:H, 0:NT]
                    for kt in range(KT):
                        pe.matmul(acc, wf_hi[:, kt, :], a_lo[:, kt, :], start=kt == 0, stop=False)
                        pe.matmul(acc, wf_hi[:, kt, :], a_hi[:, kt, :], start=False, stop=False)
                        mm = pe.matmul(acc, wf_lo[:, kt, :], a_hi[:, kt, :], start=False, stop=kt == KT - 1)
                    mm.then_inc(f_ps, 1)

            pe.wait_ge(f_lf, 1)
            for b in range(3):
                rows = min(P, NT - b * P)
                mm = pe.transpose(bank[6][0:rows, H * b:H * b + H], lf[:, b * P:b * P + rows], ident[0:H, 0:H])
            mm.then_inc(lfr_ps, 1)
            pe.wait_ge(z_ready, 1)
            pe.wait_ge(ada_mods, ADA_MAIN + 1)
            for kt in range(KC):
                mm = pe.transpose(bank[4 + kt // 4][0:2 + 2 * SB, (kt % 4) * P:(kt % 4) * P + P],
                                  z_end[:, kt, :], ident[:, :])
            mm.then_inc(z_ps, 1)
            pe.wait_ge(bank_turn, BT + MT * (G_MIX + 1))

            def turn_rows(n0, n1):
                for n in range(n0, n1):
                    src, b, half = (kT, vT)[n // 6], n % 6 // 2, n % 2
                    rows = min(P, NT - b * P)
                    if n >= 4:
                        pe.wait_ge((rowT_a, rowT_d)[n % 2], (n - 4) // 2 + 1)
                    for j in range(4):
                        mm = pe.transpose(bank[n % 4][0:rows, j * P:j * P + P],
                                          src[:, 4 * half + j, b * P:b * P + rows], ident[:, :])
                    mm.then_inc(rowT_ps, 1)

            turn_rows(0, 4)
            pe.wait_ge(sums_ready, 1)
            pe.wait_ge(lfr_done, 1)
            pe.wait_ge(s_lfc, 16 * SB * NPG)
            pages = lfc[:, :, :, :]
            acc = bank[6][:, 0:SB * NPG * H].rearrange("p (s g h) -> p s g h", s=SB, g=NPG)
            pe.matmul(acc, after[:, :], pages, start=True, stop=False)
            pe.matmul(acc[:, :, 0, :], ones[:, 0:P], pages[:, :, 1, :], start=False, stop=True).then_inc(suf_ps, 1)
            for p0 in (64, 96):
                acc = bank[7][p0:p0 + H, :]
                pe.matmul(acc[:, 0:TP], lfr[:, 0, :], upto[:, :], start=True, stop=False, tile_position=(0, p0))
                mm = pe.matmul(acc[:, P:TP], lfr[:, 1, :], upto[:, 0:P], start=False, stop=True, tile_position=(0, p0))
            mm.then_inc(cum_ps, 1)
            turn_rows(4, 8)
            pe.wait_ge(suf_done, 1)
            pe.wait_ge(cum_done, 1)
            pe.wait_ge(z_out, 1)
            for s in range(SB):
                for pg in range(NPG):
                    c0 = (s % 2) * PAST + pg * P
                    mm = pe.transpose(bank[4 + s // 2][0:H, c0:c0 + P], suf[:, s, pg, :], ident[:, :])
            mm.then_inc(sufT_ps, 1)
            turn_rows(8, 12)
            pe.wait_ge(rowT_a, 6)
            pe.wait_ge(rowT_d, 6)
            pe.wait_ge(sufT_done, 1)
            pe.wait_ge(fixed, 1)

            def scores(h, j):
                pe.wait_ge(q_ready, h + 1)
                pe.wait_ge(k_ready, h + 1)
                pe.wait_ge(qe_ready, h + 1)
                pe.wait_ge(S_max, h + 1)
                pe.matmul(bank[j][:, 0:P], q_st[j][:, 0:P], k_st[j][:, 0:P], start=True, stop=True)
                pe.matmul(bank[j][:, P:3 * P], q_st[j][:, P:TP], k_st[j][:, :], start=True, stop=True,
                          skip_group_check=True).then_inc(S_ps, 1)

            def prompt_turn(h, j):
                pe.wait_ge(S_norm, h + 1)
                pe.wait_ge(PT_out, h + 1)
                for b in range(3):
                    mm = pe.transpose(bank[2][:, b * P:b * P + P], s_p[j][:, b * P:b * P + P], ident[:, :])
                mm.then_inc(PT_ps, 1)

            def prompt_out(h, j, pair, buf):
                pe.wait_ge(PT_out, h + 2)
                pe.wait_ge(v_ready, pair + 1)
                if j == 0:
                    pe.wait_ge(O_lo, pair + 1)
                acc, c0 = bank[3][DH * j:DH * j + DH, :], DH * j
                pe.matmul(acc[:, 0:TP], v_st[buf][:, 0, c0:c0 + DH], pT_p[:, 0:TP], start=True, stop=False,
                          tile_position=(0, DH * j))
                pe.matmul(acc[:, P:TP], v_st[buf][:, 1, c0:c0 + DH], pT_p[:, TP:3 * P], start=False, stop=True,
                          tile_position=(0, DH * j)).then_inc(O_ps, 1)

            def turn_k(turn, j, ns):
                s = 2 * turn + j
                if ns[0] == 0:
                    pe.wait_ge(raw_full[2 * j], 16 * (R_PAGES + NPG * (turn + 1)))
                for n in ns:
                    if n == 2:
                        pe.wait_ge(sK_a, 2 * s + 1)
                    if n == 3:
                        pe.wait_ge(sK_d, 2 * s + 1)
                    for f in range(4):
                        a = 2 * (n // 2) + n % 2
                        mm = pe.transpose(bank[4 + n % 2][:, f * P:f * P + P], raw[2 * j][:, a, f * P:f * P + P],
                                          ident[:, :])
                    mm.then_inc(sK_ps, 1)

            def sample_scores(s, j):
                pe.wait_ge(sK_a, 2 * s + 2)
                pe.wait_ge(sK_d, 2 * s + 2)
                pe.wait_ge(sQ, s + 1)
                pe.wait_ge(sSel, s + 1)
                pe.wait_ge(sS_max, s + 1)
                for hf in range(2):
                    for q4 in range(4):
                        acc = bank[6 + hf][32 * q4:32 * q4 + 32, 0:PAST + TS]
                        pe.matmul(acc, q_bd[:, 4 * hf + q4, :], KTs[j][:, 4 * hf + q4, :], start=True, stop=False,
                                  tile_position=(0, 32 * q4))
                    for q4 in range(4):
                        acc = bank[6 + hf][32 * q4:32 * q4 + 32, 0:PAST + TS]
                        mm = pe.matmul(acc, selq[:, 4 * hf + q4, :], cumk_s[:, :], start=False, stop=True,
                                       tile_position=(0, 32 * q4))
                    mm.then_inc(sS_ps, 1)

            def pair_and_sequence(turn, j, more):
                s = 2 * turn + j
                prompt_turn(2 * s, 0)
                if more:
                    turn_k(turn + j, 1 - j, (0,))
                    pe.wait_ge(sO_lo, s + 1)
                    turn_k(turn + j, 1 - j, (1,))
                prompt_out(2 * s, 0, s, j)
                if more:
                    turn_k(turn + j, 1 - j, (2, 3))
                prompt_turn(2 * s + 1, 1)
                prompt_out(2 * s + 1, 1, s, j)
                if more:
                    scores(2 * s + 2, 0)
                pe.wait_ge(sS_norm, s + 1)
                if more:
                    pe.wait_ge(sK_a, 2 * s + 4)
                    pe.wait_ge(sK_d, 2 * s + 4)
                for hf in range(2):
                    for pg in range(2):
                        pe.transpose(bank[4 + hf][:, pg * P:pg * P + P], s_s[:, hf, pg * P:pg * P + P], ident[:, :])
                    mm = pe.transpose(bank[4 + hf][0:TS, 2 * P:3 * P], s_s[:, hf, PAST:PAST + TS], ident[:, :])
                mm.then_inc(sP_ps, 1)
                if more:
                    scores(2 * s + 3, 1)
                    sample_scores(s + 1, 1 - j)
                pe.wait_ge(sP_out, s + 2)
                pe.wait_ge(raw_full[2 * j + 1], 16 * (R_PAGES + NPG * (turn + 1)))
                for hf in range(2):
                    for blk in range(3):
                        for q4 in range(4):
                            acc = bank[4][32 * q4:32 * q4 + 32, hf * P:hf * P + P]
                            ft = 4 * hf + q4
                            if blk < 2:
                                lhs = pT_s[:, hf, blk * P + 32 * q4:blk * P + 32 * q4 + 32]
                                rhs = raw[2 * j + 1][:, 2 * blk + ft // 4, (ft % 4) * P:(ft % 4) * P + P]
                            else:
                                lhs = pT_s[0:TS, hf, 2 * P + 32 * q4:2 * P + 32 * q4 + 32]
                                rhs = v_new[0:TS, ft * P:ft * P + P]
                            mm = pe.matmul(acc, lhs, rhs, start=blk == 0, stop=blk == 2,
                                           tile_position=(0, 32 * q4), skip_group_check=True)
                mm.then_inc(page_used, 1)
                pe.wait_ge(sO_sb, s + 1)
                for hf in range(2):
                    mm = pe.transpose(bank[5][:, hf * P:hf * P + P], o_s[:, hf, :], ident[:, :])
                mm.then_inc(sOT, 1)

            turn_k(0, 0, (0, 1, 2, 3))
            scores(0, 0)
            scores(1, 1)
            sample_scores(0, 0)
            with pe.Fori(0, PAGE_TURNS - 1) as i:
                for j in range(2):
                    pair_and_sequence(i, j, True)
            pair_and_sequence(PAGE_TURNS - 1, 0, True)
            pair_and_sequence(PAGE_TURNS - 1, 1, False)

            pe.wait_ge(O_lo, SB + 1)
            pe.wait_ge(sO_lo, SB + 1)
            with pe.Fori(0, MIXES) as i:
                for t in range(PER_MIX):
                    n = N_MIX + PER_MIX * i + t
                    g = G_MIX + 4 * i
                    if t < 4:
                        product(n, t == 0, t == 3, g, SK * t, a_hi, a_lo, t % SPLIT)
                    elif t < 6:
                        product(n, t == 4, t == 5, g + 1, SK * (t - 4), o_hi, o_lo, t % SPLIT)
                    elif t < 10:
                        product(n, t == 6, t == 9, g + 2, SK * (t - 6), a_hi, a_lo, t % SPLIT)
                    else:
                        if t == 10:
                            pe.wait_ge(act_lo, 4 + 2)
                        product(n, t == 10, t == 11, g + 3, SK * (t - 10), y_hi, y_lo, t % SPLIT)
            with pe.Fori(0, MIXES) as i:
                for t in range(PER_O):
                    pe.wait_ge(act_lo, 6 + t + 1)
                    product(N_O + PER_O * i + t, t == 0, t == 3, G_O + i, SK * t, a_hi, a_lo, t % SPLIT)
                    if t:
                        ada_beside(ADA_MAIN + i, (0, 1, 3)[t - 1], ada_o)
            def sum_partitions(n):
                pe.wait_ge(sqr_done, 1 + n)
                pe.matmul(bank[7][:, 0:NT], ones[:, 0:P], sqr[:, :], start=True, stop=True).then_inc(ms_ps, 1)

            sum_partitions(MIXES)
            pe.wait_ge(ms_done, 2)
            for c in range(4):
                sum_squares(c, 4 + MIXES + c, (sq4, sq4b)[c % 2])
            with pe.Fori(0, F1S) as i:
                for t in range(PER_F1):
                    pe.wait_ge(act_lo, 10 + t % 4 + 1)
                    product(N_F1 + PER_F1 * i + t, t % 4 == 0, t % 4 == 3, G_F1 + 2 * i + t // 4,
                            SK * (t % 4), a_hi, a_lo, t % SPLIT)
            with pe.Fori(0, 2) as i:
                for t in range(PER_F2):
                    k = KF // SK
                    pe.wait_ge(act_lo, 14 + PER_F2 * i + t + 1)
                    product(N_F2 + PER_F2 * i + t, t % k == 0, t % k == k - 1, G_F2 + 2 * i + t // k,
                            SK * (t % 4), a_hi, a_lo, t % SPLIT)
            sum_partitions(2 * MIXES)
            n = 0
            for c in range(4):
                pe.wait_ge(x_upd, 4 + c + 1)
                for b in range(3):
                    rows = min(P, NT - b * P)
                    if n >= 4:
                        pe.wait_ge(y_out, n - 3)
                    for j in range(4):
                        mm = pe.transpose(bank[n % 4][0:rows, j * P:j * P + P],
                                          xT[:, 4 * c + j, b * P:b * P + rows], ident[:, :])
                    mm.then_inc(y_ps, 1)
                    n += 1

        @block.scalar
        def _(act):
            own = Own(act, own_act)
            act.sem_inc(ada_copied, 1)
            act.sem_inc(sP_out, 1)
            act.sem_inc(PT_out, 1)

            def split_hi(n, s, use, buf):
                act.wait_ge(raw_full[s], 16 * use)
                act.wait_ge(mm_turn, MT * n + MT)
                nc.scalar.copy(w_hi[buf][:, :, :], raw[s][:, :, :]).then_inc(hi_done, 1)

            def groups_done(n, mt):
                act.wait_ge(mm_turn, MT * SPLIT + MT * n + mt + 1)

            act.dma_start(c_rows[0:1, :], c_prompt).then_inc(s_c, 16)
            act.dma_start(c_rows[1:NC, :], c_sample).then_inc(s_c, 16)
            for n, g in enumerate((g_pre1, g_post1, g_pre2, g_post2)):
                act.dma_start(vec_rows[KT * n:KT * n + KT, :], g[0].rearrange("(k p) -> k p", p=P)).then_inc(s_rows, 16)
            act.dma_start(vec_rows[4 * KT:4 * KT + CW * KC, :],
                          w_conv[0].rearrange("c (k p) -> (c k) p", p=P)).then_inc(s_rows, 16)
            act.dma_start(b_rows[:, :], b_ada[0].rearrange("(k p) -> k p", p=P)).then_inc(s_rows, 16)
            act.dma_start(st_rows[:, :], state_conv[0].rearrange("s t n -> (s t) n")).then_inc(s_rows, 16)
            act.dma_start(bf[:, :], b_f[0].rearrange("(h a) -> h a", a=1)).then_inc(s_rows, 16)
            for b in range(2):
                act.dma_start(x_rows[:, b, :], x_prompt[0, b * P:b * P + P, :]).then_inc(s_x, 16)
            act.dma_start(x_rows[0:TS, 2, :], x_sample.rearrange("s t n -> (s t) n")).then_inc(s_x, 16)
            act.dma_start(table[0:1, :], page_table.rearrange("(a s) g -> a (s g)", a=1)).then_inc(s_table, 16)
            act.dma_start(wf[:, :, :], w_in[0, :, CF:CF + H].rearrange("(k p) n -> p k n", p=P)).then_inc(s_wf, 16)

            act.wait_ge(s_c, 32)
            nc.scalar.activation(c_sig[:, :], c_rows[:, :], ACT.Sigmoid).then_inc(c_sigm, 1)

            def copy_ada(g):
                act.wait_ge(ada_turn, RAW + SK * g + SK)
                act.wait_ge(ada_T, g + 1)
                nc.scalar.copy(ada_sb[:, :], bank[4][:, :]).then_inc(ada_copied, 1)

            def split_act(src, kt, dst, kd, tiles=SK):
                nc.scalar.copy(dst[:, kd:kd + tiles, :], src[:, bass.ds(kt, tiles), :]).then_inc(act_hi, 1)

            def split_h(c):
                act.wait_ge(x_upd, c + 1)
                split_act(xn, SK * c, a_hi, SK * c)

            def inverse_root(n):
                nc.scalar.preload_act_table_set("natural_log_exp_and_others")
                act.wait_ge(ms_done, n)
                own.mark(nc.scalar.activation(rstd[:, :], sq4[:, 1, :], ACT.Ln))
                own.wait()
                nc.scalar.activation(rstd[:, :], rstd[:, :], ACT.Exp, scale=-0.5).then_inc(root_done, 1)

            for g in range(ADA_FIRST):
                copy_ada(g)
                if g < 4:
                    act.wait_ge(bank_turn, SK * g + SK)
                    if g:
                        act.wait_ge(ms_ps, g)
                    nc.scalar.activation(sq4[:, :, :], xT[:, SK * g:SK * g + SK, :], ACT.Square).then_inc(sq_done, 1)
                if g == 4:
                    inverse_root(1)
                    act.wait_ge(s_wf, 16)
                    nc.scalar.copy(wf_hi[:, :, :], wf[:, :, :]).then_inc(wf_hi_done, 1)
                if g == 5:
                    split_h(0)
                    split_h(1)
                if g == 6:
                    act.wait_ge(x_ps, KT)
                    split_hi(0, 0, 1, 0)
            split_h(2)
            split_h(3)
            def half_body(i, n0, names, a0, more):
                for t in range(PER_HALF):
                    if t < PER_HALF - 1 or more:
                        split_hi(n0 + PER_HALF * i + t + 1, (t + 1) % RAW, n0 // RAW + 3 * i + (t + 1) // RAW + 1,
                                 (t + 1) % SPLIT)
                    name = names[t // 4]
                    if t % 4 == 3 and name in "uqkv":
                        dst = {"u": u_t, "q": qT, "k": kT, "v": vT}[name]
                        for mt in range(MT):
                            groups_done(n0 + PER_HALF * i + t, mt)
                            kt = mt if name == "u" else 4 * i + mt
                            nc.scalar.copy(dst[:, bass.ds(kt, 1), :].rearrange("p a n -> p (a n)"),
                                           bank[mt][:, 0:NT]).then_inc(bank_turn, 1)
                    if t % 4 == 2:
                        copy_ada(a0 + ADA_PER_HALF * i + t // 4)

            with act.Fori(0, HALVES) as i:
                half_body(i, N_UCB, "uCB", ADA_FIRST, True)
            act.wait_ge(f_z, 1)
            own.mark(nc.scalar.activation(lfe[:, :], lfe[:, :], ACT.Exp))
            own.wait()
            nc.scalar.activation(lfe[:, :], lfe[:, :], ACT.Ln, bias=1.0).then_inc(f_ln, 1)
            act.wait_ge(z_ready, 1)
            for i in range(HALVES):
                half_body(i, N_QKV, "qkv", ADA_FIRST + HALVES * ADA_PER_HALF, i < HALVES - 1)

            copy_rows(act, nc.scalar.copy, rowT_a, 0)
            act.wait_ge(rowT_ps, 12)
            for j in range(2):
                nc.scalar.copy(KTs[j][:, :, PAST:PAST + TS], kT[:, :, TP:NT])
            act.wait_ge(sufT_ps, 1)
            act.wait_ge(cleared, 1)
            for b in range(4):
                ins = nc.scalar.copy(cumk[0:H, 2 * b:2 * b + 2, 0:PAST],
                                     bank[4 + b][0:H, :].rearrange("p (s n) -> p s n", s=2))
            ins.then_inc(sufT_done, 1)
            act.wait_ge(s_kout, 32)

            def copy_q(pair, j):
                h = 2 * pair + j
                act.wait_ge(S_max, h + 1)
                nc.scalar.mul(q_st[j][0:DH, :], qT[DH * j:DH * j + DH, bass.ds(pair, 1), 0:TP].rearrange(
                    "p a n -> p (a n)"), SCALE).then_inc(q_ready, 1)

            def exp_head(h, j):
                act.wait_ge(S_max, h + 3)
                nc.scalar.activation(s_p[j][:, 0:P], s_p[j][:, 0:P], ACT.Exp, bias=small[:, 4 * j:4 * j + 1],
                                     accum_out=small[:, 4 * j + 2:4 * j + 3])
                nc.scalar.activation(s_p[j][:, P:3 * P], s_p[j][:, P:3 * P], ACT.Exp,
                                     bias=small[:, 4 * j + 1:4 * j + 2],
                                     accum_out=small[:, 4 * j + 3:4 * j + 4]).then_inc(S_exp, 1)

            def copy_pT(h):
                act.wait_ge(PT_ps, h + 1)
                act.wait_ge(O_ps, h + 1)
                nc.scalar.copy(pT_p[:, :], bank[2][:, 0:3 * P]).then_inc(PT_out, 1)

            def copy_q_bd(s):
                act.wait_ge(sS_ps, 2 * s + 1)
                tok = bass.ds(TP + ST * s, ST)
                nc.scalar.mul(q_bd[0:DH, :, 0:ST], qT[0:DH, :, tok], SCALE)
                nc.scalar.mul(q_bd[DH:P, :, ST:2 * ST], qT[DH:P, :, tok], SCALE).then_inc(sQ, 1)

            def copy_KT(s, j, n):
                act.wait_ge(sK_ps, 2 * 4 + 4 * s + n + 1)
                nc.scalar.copy(KTs[j][:, 0:4, (n // 2) * P:(n // 2) * P + P],
                               bank[4][:, :].rearrange("p (f n) -> p f n", f=4)).then_inc(sK_a, 1)

            def exp_sample(s):
                act.wait_ge(sS_max, s + 2)
                nc.scalar.activation(s_s[:, 0, :], s_s[:, 0, :], ACT.Exp, bias=small[:, 8:9],
                                     accum_out=small[:, 10:11])
                nc.scalar.activation(s_s[:, 1, :], s_s[:, 1, :], ACT.Exp, bias=small[:, 9:10],
                                     accum_out=small[:, 11:12]).then_inc(sS_exp, 1)

            def pair_and_sequence(turn, j, more):
                s = 2 * turn + j
                copy_pT(2 * s)
                if more:
                    copy_KT(s + 1, 1 - j, 0)
                exp_sample(s)
                if more:
                    copy_KT(s + 1, 1 - j, 2)
                    copy_q(s + 1, 0)
                copy_pT(2 * s + 1)
                if more:
                    copy_q(s + 1, 1)
                    copy_q_bd(s + 1)
                act.wait_ge(O_ps, 2 * s + 3)
                nc.scalar.copy(o_hi[:, bass.ds(s, 1), 0:TP].rearrange("p a n -> p (a n)"),
                               bank[3][:, 0:TP]).then_inc(O_hi, 1)
                act.wait_ge(sP_ps, s + 1)
                act.wait_ge(page_used, s + 2)
                for hf in range(2):
                    nc.scalar.copy(pT_s[:, hf, 0:2 * P], bank[4 + hf][:, 0:2 * P])
                    ins = nc.scalar.copy(pT_s[0:TS, hf, 2 * P:3 * P], bank[4 + hf][0:TS, 2 * P:3 * P])
                ins.then_inc(sP_out, 1)
                if not more:
                    act.wait_ge(s_out, 16 * 5)
                    act.wait_ge(v_ready, SB)
                    split_hi(N_MIX, 0, R_MIX + 1, 0)
                if more:
                    exp_head(2 * s + 2, 0)
                    exp_head(2 * s + 3, 1)
                act.wait_ge(page_used, s + 3)
                act.wait_ge(sOT, s + 1)
                nc.scalar.copy(o_s[:, :, :], bank[4][:, 0:2 * P].rearrange("p (a n) -> p a n", a=2)
                               ).then_inc(sO_sb, 1)
                act.wait_ge(sOT, s + 2)
                tok = bass.ds(TP + ST * s, ST)
                for e in range(2):
                    rows = slice(DH * e, DH * e + DH)
                    src = bank[5][rows, 0:2 * P].rearrange("p (k c) -> p k c", c=32)
                    ins = nc.scalar.copy(o_hi[rows, :, tok], src[:, :, ST * e:ST * e + ST])
                ins.then_inc(sO_hi, 1)

            copy_q(0, 0)
            copy_q(0, 1)
            copy_q_bd(0)
            copy_KT(0, 0, 0)
            copy_KT(0, 0, 2)
            exp_head(0, 0)
            exp_head(1, 1)
            with act.Fori(0, PAGE_TURNS - 1) as i:
                for j in range(2):
                    pair_and_sequence(i, j, True)
            pair_and_sequence(PAGE_TURNS - 1, 0, True)
            pair_and_sequence(PAGE_TURNS - 1, 1, False)

            act.wait_ge(O_lo, SB + 1)
            act.wait_ge(sO_lo, SB + 1)
            act.wait_ge(sOT, SB + 1)
            for c in range(2):
                split_act(yT, SK * c, y_hi, SK * c)
            def split_m(c):
                act.wait_ge(mm_turn, MT * (SPLIT + N_O - PER_MIX // 2 + c + 1))
                act.wait_ge(m_done, c + 2)
                split_act(m_T, SK * c, a_hi, SK * c)

            def mix_turn(i, last):
                for t in range(PER_MIX):
                    n = N_MIX + PER_MIX * i + t
                    split_hi(n + 1, (t + 1) % RAW, R_MIX + 3 * i + (t + 1) // RAW + 1, (t + 1) % SPLIT)
                    if t in (3, 9):
                        if t == 9:
                            act.wait_ge(m_done, i + 1)
                        for mt in range(MT):
                            groups_done(n, mt)
                            nc.scalar.activation((gate_a if t == 3 else gate_b)[:, mt, :], bank[mt][:, 0:NT],
                                                 ACT.Sigmoid).then_inc(bank_turn, 1)
                    if last and t == 10:
                        for c in range(3):
                            split_m(c)

            with act.Fori(0, MIXES - 1) as i:
                mix_turn(i, False)
            mix_turn(MIXES - 1, True)
            split_m(3)

            def gated(dst, n, i, done):
                act.wait_ge(sqr_done, done + 1)
                for mt in range(MT):
                    groups_done(n, mt)
                    kt = bass.ds(MT * i + mt, 1)
                    ins = nc.scalar.activation(sq4[:, mt, :], bank[mt][:, 0:NT], ACT.Square)
                    if mt == MT - 1:
                        ins.then_inc(sq_done, 1)
                    nc.scalar.activation(dst[:, kt, 0:TP].rearrange("p a n -> p (a n)"), bank[mt][:, 0:TP],
                                         ACT.Identity, scale=modG[:, kt, 0:1].rearrange("p a n -> p (a n)"))
                    nc.scalar.copy(dst[:, kt, TP:NT].rearrange("p a n -> p (a n)"),
                                   bank[mt][:, TP:NT]).then_inc(bank_turn, 1)

            with act.Fori(0, MIXES) as i:
                for t in range(PER_O):
                    split_hi(N_O + PER_O * i + t + 1, (t + 1) % RAW, R_O + i + (t + 1) // RAW + 1, (t + 1) % SPLIT)
                    if t == 2:
                        copy_ada(ADA_MAIN + i)
                gated(r_T, N_O + PER_O * i + PER_O - 1, i, i)
            inverse_root(2)

            def square_x1(c):
                act.wait_ge(x1_done, c + 1)
                if c >= 2:
                    act.wait_ge(ms_ps, 4 + 1 + c - 1)
                nc.scalar.activation((sq4, sq4b)[c % 2][:, :, :], xT[:, SK * c:SK * c + SK, :],
                                     ACT.Square).then_inc(sq_done, 1)

            def scale_x1(c):
                for kt in range(SK * c, SK * c + SK):
                    ins = nc.scalar.activation(x1A[:, kt, 0:TP], xT[:, kt, 0:TP], ACT.Identity,
                                               scale=modA[:, kt, 0:1])
                ins.then_inc(x1A_done, 1)

            def split_h2(c):
                k0 = SK * c
                act.wait_ge(f_done, c + 1)
                for kt in range(k0, k0 + SK):
                    nc.scalar.activation(a_hi[:, kt, 0:TP], x1A[:, kt, 0:TP], ACT.Identity,
                                         bias=mods[:, 3 * KT + kt, 0:1])
                nc.scalar.copy(a_hi[:, k0:k0 + SK, TP:NT], x1A[:, k0:k0 + SK, TP:NT]).then_inc(act_hi, 1)

            square_x1(0)
            scale_x1(0)
            for c in range(1, 4):
                square_x1(c)
            scale_x1(1)
            inverse_root(3)
            nc.scalar.preload_act_table(ACT.Sigmoid)
            scale_x1(2)
            split_h2(0)
            scale_x1(3)
            split_h2(1)
            def f1_turn(i, first):
                for t in range(PER_F1):
                    n = N_F1 + PER_F1 * i + t
                    split_hi(n + 1, (t + 1) % RAW, R_F1 + 2 * i + (t + 1) // RAW + 1, (t + 1) % SPLIT)
                    if first and t < 2:
                        split_h2(2 + t)
                    if t == 3:
                        act.wait_ge(bank_turn, BT + MT * (G_F1 + 2 * i + 1))
                        for mt in range(MT):
                            groups_done(n, mt)
                            nc.scalar.activation(sg[:, mt, :], bank[mt][:, 0:NT], ACT.Sigmoid).then_inc(gate_done, 1)

            f1_turn(0, True)
            with act.Fori(1, F1S) as i:
                f1_turn(i, False)
            k = KF // SK
            for c in range(2):
                act.wait_ge(mm_turn, MT * (SPLIT + N_F2 - SK + c + 1))
                act.wait_ge(bank_turn, BT + MT * (G_F1 + 2 * (c + 1) + 1))
                split_act(hid, SK * c, a_hi, SK * c)

            def f2_body(i, more):
                for t in range(PER_F2):
                    n = N_F2 + PER_F2 * i + t
                    if t < PER_F2 - 1:
                        split_hi(n + 1, (t + 1) % RAW, R_F2 + [6, 6, 5, 5][(t + 1) % RAW] * i + (t + 1) // RAW + 1,
                                 (t + 1) % SPLIT)
                    elif more:
                        split_hi(n + 1, 0, R_F2 + 6 * (i + 1) + 1, 0)
                    if t % k == k - 1:
                        gated(f_T, n, 2 * i + t // k, MIXES + 2 * i + t // k)
                    if t < PER_F2 - 2 or more:
                        t2 = (t + 2) % PER_F2
                        last = n - 2 if t + 2 < PER_F2 else N_F2 + PER_F2 * i + 20 + t2
                        act.wait_ge(mm_turn, MT * (SPLIT + last + 1))
                        split_act(hid, SK * (t2 % k), a_hi, SK * (t2 % 4))

            for i in range(2):
                f2_body(i, i == 0)
            inverse_root(4)
            n = 0
            for c in range(4):
                for b in range(3):
                    rows = min(P, NT - b * P)
                    act.wait_ge(y_ps, n + 1)
                    nc.scalar.copy(y_rows[0:rows, b, SN * c:SN * c + SN], bank[n % 4][0:rows, :]).then_inc(y_out, 1)
                    n += 1

        @block.vector
        def _(dve):
            own = Own(dve, own_dve)
            tt, ts, stt = nc.vector.tensor_tensor, nc.vector.tensor_scalar, nc.vector.scalar_tensor_tensor

            def split_lo(n, s, buf):
                dve.wait_ge(hi_done, n + 1)
                tt(w_lo[buf][:, :, :], raw[s][:, :, :], w_hi[buf][:, :, :].bitcast(F32),
                   ALU.subtract).then_inc(raw_turn, 1)

            def groups_done(n, mt):
                dve.wait_ge(mm_turn, MT * SPLIT + MT * n + mt + 1)

            def seqs(ap, kts):
                return ap.rearrange("p k (s t) -> p k s t", s=SB)

            def cond(tile, k0, kts):
                return tile[:, k0:k0 + kts, 1:NC].unsqueeze(3).broadcast_to([P, kts, SB, ST])

            dve.sem_inc(raw_turn, RAW)
            dve.sem_inc(m_done, 1)
            dve.sem_inc(sqr_done, 1)
            dve.sem_inc(ada_mods, 1)
            dve.sem_inc(S_max, 2)
            dve.sem_inc(O_lo, 1)
            dve.sem_inc(sO_lo, 1)
            dve.sem_inc(sS_max, 1)
            own.mark(nc.vector.memset(cT[:, :, :], 0.0))
            dve.wait_ge(c_sigm, 1)
            tt(c_rows[:, :], c_rows[:, :], c_sig[:, :], ALU.mult).then_inc(c_silu, 1)
            dve.wait_ge(cT_ps, 1)
            own.wait()
            nc.vector.tensor_copy(cT[:, :, 0:NC], bank[6][:, 0:KT * NC].rearrange("p (k r) -> p k r", k=KT)
                                  ).then_inc(cT_ready, 1)
            dve.wait_ge(rows_ps, 1)
            nv, nb = 4 * KT + CW * KC, NMOD * KT
            own.mark(nc.vector.tensor_copy(vecT[:, :], bank[4][:, 0:nv]))
            own.mark(nc.vector.tensor_copy(bT[:, :], bank[4][:, P:P + nb]))
            nc.vector.tensor_copy(st_T[:, :, :, :], bank[5][:, 0:KC * SB * 2].rearrange(
                "p (k s t) -> p k s t", k=KC, s=SB)).then_inc(vec_ready, 1)
            dve.wait_ge(m4_ps, 1)
            own.mark(nc.vector.memset(mask_s[:, :], MASKED))
            own.wait()
            nc.vector.tensor_copy(mask_s[:, :].rearrange("p (s c) -> p s c", s=SB)[:, :, 0:ST],
                                  bank[7][:, 0:ST].unsqueeze(1).broadcast_to([P, SB, ST])).then_inc(m4_done, 1)
            dve.wait_ge(consts, 3)
            own.mark(nc.vector.tensor_copy(sel[32:32 + H, :, :], sel[0:H, :, :]))
            own.wait()
            nc.vector.tensor_copy(selq[:, :, 0:2 * ST], sel[:, :, :]).then_inc(pool_sel, 1)

            def copy_x(kt):
                dve.wait_ge(x_ps, kt + 1)
                nc.vector.tensor_copy(xT[:, kt, :], bank[kt % 4][:, 0:NT]).then_inc(bank_turn, 1)

            def mean_square(n):
                dve.wait_ge(ms_ps, n)
                ts(sq4[:, 1, :], bank[7][:, 0:NT], 1.0 / D, EPS, ALU.mult, ALU.add).then_inc(ms_done, 1)

            def refine_root(n):
                dve.wait_ge(root_done, n)
                own.mark(tt(sq4[:, 0, :], rstd[:, :], rstd[:, :], ALU.mult))
                own.wait()
                own.mark(stt(sq4[:, 0, :], sq4[:, 0, :], -0.5, sq4[:, 1, :], ALU.mult, ALU.mult))
                own.wait()
                stt(rstd[:, :], sq4[:, 0, :], 1.5, rstd[:, :], ALU.add, ALU.mult).then_inc(rstd_ready, 1)
                dve.wait_ge(rstd_ready, n)

            def times_rstd(dst, src, c):
                own.mark(tt(dst[:, SK * c:SK * c + SK, :], src[:, SK * c:SK * c + SK, :],
                            rstd[:, :].unsqueeze(1).broadcast_to([P, SK, NT]), ALU.mult))

            def modulate(dst, A, S0, c):
                own.wait()
                k0 = SK * c
                own.mark(tt(seqs(dst[:, k0:k0 + SK, TP:NT], SK), seqs(dst[:, k0:k0 + SK, TP:NT], SK),
                            cond(A, k0, SK), ALU.mult))
                for kt in range(k0, k0 + SK):
                    own.mark(ts(dst[:, kt, 0:TP], dst[:, kt, 0:TP], A[:, kt, 0:1], mods[:, S0 + kt, 0:1],
                                ALU.mult, ALU.add))
                own.wait()
                return tt(seqs(dst[:, k0:k0 + SK, TP:NT], SK), seqs(dst[:, k0:k0 + SK, TP:NT], SK),
                          cond(mods, S0 + k0, SK), ALU.add)

            def add_ada(n, g):
                dve.wait_ge(ada_T, n + 2)
                src = bank[5][:, :].rearrange("p (m j r) -> p m r j", m=MT, j=4)[:, :, 0:NC, :]
                nc.vector.tensor_reduce(mods[:, bass.ds(MT * g, MT), :], src, AX.X, ALU.add).then_inc(ada_mods, 1)

            def add_bias(lo_, hi_):
                own.mark(tt(mods[:, lo_:hi_, :], mods[:, lo_:hi_, :],
                            bT[:, lo_:hi_].unsqueeze(2).broadcast_to([P, hi_ - lo_, NC]), ALU.add))
                own.wait()

            def scaled(dst, g0, part, plus, k0=0, k1=KT):
                own.mark(stt(dst[:, k0:k1, :], mods[:, part * KT + k0:part * KT + k1, :], plus,
                             vecT[:, g0 + k0:g0 + k1].unsqueeze(2).broadcast_to([P, k1 - k0, NC]), ALU.add, ALU.mult))
                own.wait()

            def split_act_lo(n, src, kt, hi, lo, kd):
                dve.wait_ge(act_hi, n + 1)
                tt(lo[:, kd:kd + SK, :], src[:, bass.ds(kt, SK), :], hi[:, kd:kd + SK, :].bitcast(F32),
                   ALU.subtract).then_inc(act_lo, 1)

            def make_h(c):
                k0 = SK * c
                own.wait()
                add_bias(k0, k0 + SK)
                add_bias(KT + k0, KT + k0 + SK)
                scaled(modA, 0, 1, 1.0, k0, k0 + SK)
                modulate(xn, modA, 0, c).then_inc(x_upd, 1)

            for n in range(ADA_FIRST):
                if n < 2:
                    for kt in range(KT // 2 * n, KT // 2 * (n + 1)):
                        copy_x(kt)
                g = n // 2 + SK * (n % 2)
                ins = add_ada(n, g)
                if n == 4:
                    mean_square(4)
                if n == 5:
                    refine_root(1)
                    for c in range(4):
                        times_rstd(xn, xT, c)
                    dve.wait_ge(wf_hi_done, 1)
                    tt(wf_lo[:, :, :], wf[:, :, :], wf_hi[:, :, :].bitcast(F32), ALU.subtract).then_inc(wf_split, 1)
                    dve.wait_ge(ada_mods, n + 2)
                    for c in range(2):
                        make_h(c)
                    for c in range(2):
                        split_act_lo(c, xn, SK * c, a_hi, a_lo, SK * c)
                if n == 6:
                    make_h(2)
                    split_lo(0, 0, 0)
            dve.wait_ge(ada_mods, ADA_FIRST + 1)
            make_h(3)
            for c in range(2, 4):
                split_act_lo(c, xn, SK * c, a_hi, a_lo, SK * c)
            dve.wait_ge(act_lo, 4)
            own.mark(nc.vector.memset(z_p[:, :, 0:CW - 1], 0.0))
            own.mark(nc.vector.tensor_copy(z_s[:, :, :, 0:CW - 1],
                                           st_T[:, :, :, :]))
            def half_body(i, n0, names, a0, more):
                for t in range(PER_HALF):
                    n = n0 + PER_HALF * i + t
                    if t < PER_HALF - 1 or more:
                        split_lo(n + 1, (t + 1) % RAW, (t + 1) % SPLIT)
                    name = names[t // 4]
                    if name == "C" and t % 4 == 3:
                        for mt in range(MT):
                            groups_done(n, mt)
                            kt = bass.ds(4 * i + mt, 1)
                            own.mark(tt(z_p[:, kt, CW - 1:CW - 1 + TP].rearrange("p a n -> p (a n)"),
                                        bank[mt][:, 0:TP], u_t[:, mt, 0:TP], ALU.mult))
                            tt(z_s[:, kt, :, CW - 1:CW - 1 + ST].rearrange("p a s t -> p (a s) t"),
                               bank[mt][:, TP:NT].rearrange("p (s t) -> p s t", s=SB),
                               u_t[:, mt, TP:NT].rearrange("p (s t) -> p s t", s=SB), ALU.mult).then_inc(bank_turn, 1)
                    if name == "B":
                        mt = t % 4
                        if mt == 0:
                            dve.wait_ge(bank_turn, BT + MT * (G_UCB + 3 * i + 3))
                            own.wait()
                        kt = bass.ds(4 * i + mt, 1)

                        def wc(tap):
                            return vecT[:, bass.ds(4 * KT + tap * KC + 4 * i + mt, 1)]
                        c_p = conv[:, mt, 0:TP]
                        c_s = conv[:, mt, TP:NT].rearrange("p (s t) -> p s t", s=SB)

                        def z_at(tap):
                            return (z_p[:, kt, tap:tap + TP].rearrange("p a n -> p (a n)"),
                                    z_s[:, kt, :, tap:tap + ST].rearrange("p a s t -> p (a s) t"))
                        zp0, zs0 = z_at(0)
                        own.mark(ts(c_p, zp0, wc(0), None, ALU.mult))
                        own.mark(ts(c_s, zs0, wc(0), None, ALU.mult))
                        for tap in (1, 2):
                            zp, zs = z_at(tap)
                            own.wait()
                            own.mark(stt(c_p, zp, wc(tap), c_p, ALU.mult, ALU.add))
                            own.mark(stt(c_s, zs, wc(tap), c_s, ALU.mult, ALU.add))
                        if mt == 3:
                            own.wait()
                            for m in range(MT):
                                groups_done(n, m)
                                tt(yT[:, bass.ds(4 * i + m, 1), :].rearrange("p a n -> p (a n)"), bank[m][:, 0:NT],
                                   conv[:, m, :], ALU.mult).then_inc(bank_turn, 1)
                    if t % 4 == 3:
                        add_ada(a0 + ADA_PER_HALF * i + t // 4, a0 + ADA_PER_HALF * i + t // 4)

            with own.loop(HALVES, MT + 6 * MT) as i:
                half_body(i, N_UCB, "uCB", ADA_FIRST, True)
            own.wait()
            own.mark(nc.vector.tensor_copy(z_end[:, :, 0:2], z_p[:, :, TP:TP + 2]))
            nc.vector.tensor_copy(z_end[:, :, 2:2 + 2 * SB].rearrange("p k (s t) -> p k s t", s=SB),
                                  z_s[:, :, :, ST:ST + 2]).then_inc(z_ready, 1)
            dve.wait_ge(f_ps, 1)
            own.mark(ts(lfz[:, :], bank[6][0:H, 0:NT], bf[:, 0:1], None, ALU.add))
            own.wait()
            own.mark(ts(lfe[:, :], lfz[:, :], -1.0, None, ALU.mult))
            own.wait()
            tt(lfe[:, :], lfe[:, :], lfz[:, :], ALU.min).then_inc(f_z, 1)
            dve.wait_ge(f_ln, 1)
            stt(lf[:, :], lfz[:, :], 0.0, lfe[:, :], ALU.min, ALU.subtract).then_inc(f_lf, 1)
            for i in range(HALVES):
                half_body(i, N_QKV, "qkv", ADA_FIRST + HALVES * ADA_PER_HALF, i < HALVES - 1)
            dve.wait_ge(lfr_ps, 1)
            for b in range(3):
                rows = min(P, NT - b * P)
                ins = nc.vector.tensor_copy(lfr[0:rows, b, :], bank[6][0:rows, H * b:H * b + H])
            ins.then_inc(lfr_done, 1)
            copy_rows(dve, nc.vector.tensor_copy, rowT_d, 1, 4)
            dve.wait_ge(z_ps, 1)
            own.mark(nc.vector.tensor_copy(z_rows[:, 0:512], bank[4][0:2 + 2 * SB, :]))
            nc.vector.tensor_copy(z_rows[:, 512:DC], bank[5][0:2 + 2 * SB, :]).then_inc(z_out, 1)
            dve.wait_ge(suf_ps, 1)
            nc.vector.tensor_copy(suf[:, :, :, :], bank[6][:, 0:SB * NPG * H].rearrange(
                "p (s g h) -> p s g h", s=SB, g=NPG)).then_inc(suf_done, 1)
            dve.wait_ge(cum_ps, 1)
            dve.wait_ge(fixed, 1)
            for j in range(2):
                own.mark(ts(k_st[j][64:64 + H, :], bank[7][64:64 + H, 0:TP], -1.0, None, ALU.mult))
            own.mark(nc.vector.tensor_copy(cum_q[96:96 + H, :], bank[7][96:96 + H, 0:TP]))
            lfs = lf[:, TP:NT].rearrange("p (s t) -> p s t", s=SB)
            cqs = cq[0:H, :].rearrange("p (s t) -> p s t", s=SB)
            own.mark(nc.vector.tensor_copy(cqs[:, :, 0:1], lfs[:, :, 0:1]))
            for t in range(1, ST):
                own.wait()
                own.mark(tt(cqs[:, :, t:t + 1], cqs[:, :, t - 1:t], lfs[:, :, t:t + 1], ALU.add))
            own.wait()
            own.mark(nc.vector.tensor_copy(cq[32:32 + H, :], cq[0:H, :]))
            for s in range(SB):
                ins = ts(cumk[0:H, s, PAST:PAST + TS], cq[0:H, :], -1.0, None, ALU.mult)
            ins.then_inc(cum_done, 1)
            nc.vector.memset(q_bd[:, :, :], 0.0).then_inc(cleared, 1)
            copy_rows(dve, nc.vector.tensor_copy, rowT_d, 5)
            dve.wait_ge(ada_mods, ADA_MAIN + 1)
            add_bias(2 * KT, 5 * KT)
            scaled(modG, KT, 2, 0.0)
            scaled(modA, 2 * KT, 4, 1.0)

            def copy_k(pair, j):
                h = 2 * pair + j
                nc.vector.tensor_copy(k_st[j][0:DH, :], kT[DH * j:DH * j + DH, bass.ds(pair, 1), 0:TP].rearrange(
                    "p a n -> p (a n)")).then_inc(k_ready, 1)

            def max_head(h, j):
                dve.wait_ge(S_ps, h + 1)
                own.step()
                own.mark(nc.vector.tensor_tensor_reduce(
                    s_p[j][:, 0:P], bank[j][:, 0:P], mask_q[:, P:TP], 1.0, MASKED, ALU.add, ALU.max,
                    small[:, 4 * j:4 * j + 1]))
                own.mark(nc.vector.tensor_tensor_reduce(
                    s_p[j][:, P:3 * P], bank[j][:, P:3 * P], mask_q[:, :], 1.0, MASKED, ALU.add, ALU.max,
                    small[:, 4 * j + 1:4 * j + 2]))
                own.wait()
                ts(small[:, 4 * j:4 * j + 2], small[:, 4 * j:4 * j + 2], -1.0, None, ALU.mult).then_inc(S_max, 1)

            def norm_head(h, j):
                dve.wait_ge(S_exp, h + 1)
                own.mark(nc.vector.reciprocal(small[:, 4 * j + 2:4 * j + 4], small[:, 4 * j + 2:4 * j + 4]))
                own.wait()
                own.mark(ts(s_p[j][:, 0:P], s_p[j][:, 0:P], small[:, 4 * j + 2:4 * j + 3], None, ALU.mult))
                ts(s_p[j][:, P:3 * P], s_p[j][:, P:3 * P], small[:, 4 * j + 3:4 * j + 4], None,
                   ALU.mult).then_inc(S_norm, 1)

            def copy_KT(s, j, n):
                dve.wait_ge(sK_ps, 2 * 4 + 4 * s + n + 1)
                nc.vector.tensor_copy(KTs[j][:, 4:8, (n // 2) * P:(n // 2) * P + P],
                                      bank[5][:, :].rearrange("p (f n) -> p f n", f=4)).then_inc(sK_d, 1)

            def max_sample(s):
                dve.wait_ge(sS_ps, 2 * s + 3)
                for hf in range(2):
                    msk = mask_s[:, bass.ds(TS * s, TS)]
                    own.mark(nc.vector.tensor_copy(s_s[:, hf, 0:PAST], bank[6 + hf][:, 0:PAST]))
                    own.mark(tt(s_s[:, hf, PAST:PAST + TS], bank[6 + hf][:, PAST:PAST + TS], msk, ALU.add))
                own.wait()
                own.mark(nc.vector.tensor_reduce(small[:, 8:10], s_s[:, :, :], AX.X, ALU.max))
                own.wait()
                ts(small[:, 8:10], small[:, 8:10], -1.0, None, ALU.mult).then_inc(sS_max, 1)

            def pair_and_sequence(turn, j, more):
                s = 2 * turn + j
                if more:
                    copy_KT(s + 1, 1 - j, 1)
                    copy_KT(s + 1, 1 - j, 3)
                    copy_k(s + 1, 0)
                    copy_k(s + 1, 1)
                dve.wait_ge(sS_exp, s + 1)
                own.mark(nc.vector.reciprocal(small[:, 10:12], small[:, 10:12]))
                own.wait()
                own.mark(ts(s_s[:, 0, :], s_s[:, 0, :], small[:, 10:11], None, ALU.mult))
                ts(s_s[:, 1, :], s_s[:, 1, :], small[:, 11:12], None, ALU.mult).then_inc(sS_norm, 1)
                dve.wait_ge(O_hi, s + 1)
                at_ = bass.ds(s, 1)
                tt(o_lo[:, at_, 0:TP].rearrange("p a n -> p (a n)"), bank[3][:, 0:TP],
                   o_hi[:, at_, 0:TP].rearrange("p a n -> p (a n)").bitcast(F32), ALU.subtract).then_inc(O_lo, 1)
                if not more:
                    split_lo(N_MIX, 0, 0)
                if more:
                    max_head(2 * s + 2, 0)
                    max_head(2 * s + 3, 1)
                    norm_head(2 * s + 2, 0)
                    norm_head(2 * s + 3, 1)
                    max_sample(s + 1)
                dve.wait_ge(sO_hi, s + 1)
                tok = bass.ds(TP + ST * s, ST)
                for e in range(2):
                    rows = slice(DH * e, DH * e + DH)
                    src = bank[5][rows, 0:2 * P].rearrange("p (k c) -> p k c", c=32)
                    ins = tt(o_lo[rows, :, tok], src[:, :, ST * e:ST * e + ST], o_hi[rows, :, tok].bitcast(F32),
                             ALU.subtract)
                ins.then_inc(sO_lo, 1)

            copy_k(0, 0)
            copy_k(0, 1)
            dve.wait_ge(s_zout, 32)
            copy_KT(0, 0, 1)
            copy_KT(0, 0, 3)
            max_head(0, 0)
            max_head(1, 1)
            norm_head(0, 0)
            norm_head(1, 1)
            max_sample(0)
            with own.loop(PAGE_TURNS - 1, 2 * (2 * 2 + 2 + 2 * 3 + 5)) as i:
                for j in range(2):
                    pair_and_sequence(i, j, True)
            pair_and_sequence(PAGE_TURNS - 1, 0, True)
            pair_and_sequence(PAGE_TURNS - 1, 1, False)

            for c in range(2):
                split_act_lo(4 + c, yT, SK * c, y_hi, y_lo, SK * c)
            def mix_turn(i, last):
                for t in range(PER_MIX):
                    n = N_MIX + PER_MIX * i + t
                    split_lo(n + 1, (t + 1) % RAW, (t + 1) % SPLIT)
                    if t == 5:
                        for mt in range(MT):
                            groups_done(n, mt)
                            tt(m_T[:, bass.ds(MT * i + mt, 1), :].rearrange("p a n -> p (a n)"), bank[mt][:, 0:NT],
                               gate_a[:, mt, :], ALU.mult).then_inc(bank_turn, 1)
                    if last and t == 10:
                        for c in range(3):
                            split_act_lo(6 + c, m_T, SK * c, a_hi, a_lo, SK * c)
                    if t == 11:
                        for mt in range(MT):
                            groups_done(n, mt)
                            tt(gate_b[:, mt, :], bank[mt][:, 0:NT], gate_b[:, mt, :], ALU.mult).then_inc(bank_turn, 1)
                        dve.wait_ge(bank_turn, BT + MT * (G_MIX + 4 * i + 3 + 2))
                        m = m_T[:, bass.ds(MT * i, MT), :]
                        tt(m, m, gate_b[:, :, :], ALU.add).then_inc(m_done, 1)

            with dve.Fori(0, MIXES - 1) as i:
                mix_turn(i, False)
            mix_turn(MIXES - 1, True)
            split_act_lo(6 + 3, m_T, SK * 3, a_hi, a_lo, SK * 3)

            def add_squares(n):
                dve.wait_ge(sq_done, n)
                own.mark(nc.vector.tensor_reduce(rstd[:, :], sq4[:, :, :].rearrange("p k t -> p t k"), AX.X, ALU.add))
                own.wait()
                tt(sqr[:, :], sqr[:, :], rstd[:, :], ALU.add).then_inc(sqr_done, 1)

            own.mark(nc.vector.memset(sqr[:, :], 0.0))
            with own.loop(MIXES, 1) as i:
                for t in range(PER_O):
                    split_lo(N_O + PER_O * i + t + 1, (t + 1) % RAW, (t + 1) % SPLIT)
                add_ada(ADA_MAIN + i, ADA_MAIN + i)
                dve.wait_ge(sqr_done, i + 1)
                add_squares(4 + i + 1)

            def h2_lo(c):
                k0 = SK * c
                dve.wait_ge(act_hi, 10 + c + 1)
                for kt in range(k0, k0 + SK):
                    stt(a_lo[:, kt, 0:TP], x1A[:, kt, 0:TP], mods[:, 3 * KT + kt, 0:1],
                        a_hi[:, kt, 0:TP].bitcast(F32), ALU.add, ALU.subtract)
                tt(a_lo[:, k0:k0 + SK, TP:NT], x1A[:, k0:k0 + SK, TP:NT], a_hi[:, k0:k0 + SK, TP:NT].bitcast(F32),
                   ALU.subtract).then_inc(act_lo, 1)

            def gate_samples(dst, c):
                v = seqs(dst[:, SK * c:SK * c + SK, TP:NT], SK)
                own.mark(tt(v, v, cond(modG, SK * c, SK), ALU.mult))

            def add_normed(src, c, norms):
                v, x_ = src[:, SK * c:SK * c + SK, :], xT[:, SK * c:SK * c + SK, :]
                if c < 2:
                    own.mark(tt(v, v, rstd[:, :].unsqueeze(1).broadcast_to([P, SK, NT]), ALU.mult))
                    own.wait()
                else:
                    dve.wait_ge(normed, 2 * norms + c - 1)
                return tt(x_, x_, v, ALU.add)

            dve.wait_ge(bank_turn, BT + MT * (G_F1 + 1))
            for c in range(4):
                gate_samples(r_T, c)
            mean_square(4 + 1)
            refine_root(2)
            for c in range(4):
                add_normed(r_T, c, 0).then_inc(x1_done, 1)
                dve.wait_ge(x1_done, c + 1)
                v = seqs(x1A[:, SK * c:SK * c + SK, TP:NT], SK)
                own.mark(tt(v, seqs(xT[:, SK * c:SK * c + SK, TP:NT], SK), cond(modA, SK * c, SK), ALU.mult))
            mean_square(4 + 1 + 4)
            refine_root(3)
            def h2_times_rstd(c):
                k0 = SK * c
                dve.wait_ge(x1A_done, c + 1)
                v = x1A[:, k0:k0 + SK, :]
                own.mark(tt(v, v, rstd[:, :].unsqueeze(1).broadcast_to([P, SK, NT]), ALU.mult))
                own.wait()
                v = seqs(x1A[:, k0:k0 + SK, TP:NT], SK)
                tt(v, v, cond(mods, 3 * KT + k0, SK), ALU.add).then_inc(f_done, 1)

            h2_times_rstd(0)
            h2_times_rstd(1)
            h2_lo(0)
            h2_lo(1)

            def f1_turn(i, first, last):
                for t in range(PER_F1):
                    n = N_F1 + PER_F1 * i + t
                    split_lo(n + 1, (t + 1) % RAW, (t + 1) % SPLIT)
                    if first and t < 2:
                        h2_times_rstd(2 + t)
                        h2_lo(2 + t)
                    if first and t == 2:
                        dve.wait_ge(ada_mods, ADA_G + 1)
                        add_bias(5 * KT, NMOD * KT)
                        scaled(modG, 3 * KT, 5, 0.0)
                    if t == 3:
                        for mt in range(MT):
                            dve.wait_ge(gate_done, MT * i + mt + 1)
                            tt(sg[:, mt, :], bank[mt][:, 0:NT], sg[:, mt, :], ALU.mult).then_inc(bank_turn, 1)
                    if t == 7:
                        if last:
                            for c in range(2):
                                split_act_lo(14 + c, hid, SK * c, a_hi, a_lo, SK * c)
                        for mt in range(MT):
                            groups_done(n, mt)
                            tt(hid[:, bass.ds(MT * i + mt, 1), :].rearrange("p a n -> p (a n)"),
                               bank[mt][:, 0:NT], sg[:, mt, :], ALU.mult).then_inc(bank_turn, 1)

            f1_turn(0, True, False)
            with dve.Fori(1, F1S - 1) as i:
                f1_turn(i, False, False)
            f1_turn(F1S - 1, False, True)
            k = KF // SK
            own.mark(nc.vector.memset(sqr[:, :], 0.0))

            def add_f_squares(g):
                own.wait()
                dve.wait_ge(sqr_done, MIXES + g + 1)
                add_squares(4 + MIXES + 4 + g + 1)

            for i in range(2):
                for t in range(PER_F2):
                    if t < PER_F2 - 1:
                        split_lo(N_F2 + PER_F2 * i + t + 1, (t + 1) % RAW, (t + 1) % SPLIT)
                    elif i == 0:
                        split_lo(N_F2 + PER_F2 * i + t + 1, 0, 0)
                    if t % k == 0 and i + t > 0:
                        add_f_squares(2 * i + t // k - 1)
                    if t < PER_F2 - 2 or i == 0:
                        t2 = (t + 2) % PER_F2
                        split_act_lo(14 + PER_F2 * i + t + 2, hid, SK * (t2 % k), a_hi, a_lo, SK * (t2 % 4))
            add_f_squares(MIXES - 1)
            dve.wait_ge(bank_turn, BT + MT * (G_END + 1))
            for c in range(4):
                gate_samples(f_T, c)
            mean_square(4 + 1 + 4 + 1)
            refine_root(4)
            for c in range(4):
                add_normed(f_T, c, 1).then_inc(x_upd, 1)

        @block.gpsimd
        def _(pool):
            own = Own(pool, own_pool)
            g = nc.gpsimd
            own.mark(g.memset(ident[:, :], 0.0))
            own.mark(g.memset(m4_T[:, :], 0.0))
            own.mark(g.memset(ones[:, :], 1.0))
            own.mark(g.memset(mask_q[:, :], 0.0))
            own.mark(g.memset(sel[:, :, :], 0.0))
            own.mark(g.memset(selq[:, :, :], 0.0))
            own.wait()
            own.mark(g.affine_select(out=ident[:, :], in_=ident[:, :], compare_op=ALU.not_equal, fill=1.0, base=0,
                                     pattern=[[-1, P]], channel_multiplier=1))
            g.affine_select(out=m4_T[:, :].rearrange("j (r t) -> j r t", t=ST),
                            in_=m4_T[:, :].rearrange("j (r t) -> j r t", t=ST), compare_op=ALU.is_ge, fill=MASKED,
                            base=0, pattern=[[0, P // ST], [1, ST]], channel_multiplier=-1).then_inc(consts, 1)
            g.affine_select(out=mask_q[:, P:TP], in_=mask_q[:, P:TP], compare_op=ALU.is_ge, fill=MASKED, base=0,
                            pattern=[[-1, P]], channel_multiplier=1).then_inc(consts, 1)
            for par in range(2):
                part = sel[0:H, :, ST * par:ST * par + ST]
                ins = g.affine_select(out=part, in_=part, compare_op=ALU.not_equal, fill=1.0, base=-par,
                                      pattern=[[-2, KA], [0, ST]], channel_multiplier=1)
            ins.then_inc(consts, 1)
            pool.wait_ge(x_upd, 4)
            pool.wait_ge(s_table, 16)
            pages = lfc[:, :, :, :].rearrange("p s g h -> p (s g) h")
            with pool.Fori(0, SB * NPG) as n:
                r = pool.value_load(table[0:1, bass.ds(n, 1)], min_val=0, max_val=POOL - 1)
                pool.dma_start(pages[:, bass.ds(n, 1), :].rearrange("p a h -> p (a h)"),
                               cache_logf[0, bass.ds(r, 1), :, :].rearrange("a p h -> p (a h)")).then_inc(s_lfc, 16)
            pool.wait_ge(ada_turn, RAW + SK * ADA_MAIN)
            own.mark(g.memset(cumk[0:32, :, :], 0.0))
            own.wait()
            own.mark(g.memset(upto[:, :], 1.0))
            own.mark(g.memset(after[:, :], 1.0))
            own.wait()
            own.mark(g.affine_select(out=upto[:, 0:P], in_=upto[:, 0:P], compare_op=ALU.is_ge, fill=0.0, base=0,
                                     pattern=[[1, P]], channel_multiplier=-1))
            g.affine_select(out=after[:, :], in_=after[:, :], compare_op=ALU.is_gt, fill=0.0, base=0,
                            pattern=[[-1, P]], channel_multiplier=1).then_inc(sums_ready, 1)
            pool.wait_ge(sums_ready, 1)
            for j in range(2):
                own.wait()
                own.mark(g.memset(q_st[j][64:112, :], 0.0))
                own.wait()
                own.mark(g.memset(k_st[j][64:112, :], 0.0))
            own.wait()
            own.mark(g.memset(k_st[0][96:112, :], 1.0))
            own.wait()
            g.memset(k_st[1][96:112, :], 1.0).then_inc(fixed, 1)
            pool.wait_ge(fixed, 1)
            own.mark(g.memset(cumk[32:48, :, :], 1.0))
            pool.wait_ge(z_out, 1)
            pool.dma_start(conv_prompt[0, 0, :, :], z_rows[0:2, :]).then_inc(s_zout, 16)
            pool.dma_start(conv_sample[0].rearrange("s t n -> (s t) n"), z_rows[2:2 + 2 * SB, :]).then_inc(s_zout, 16)
            pool.wait_ge(lfr_done, 1)
            for b in range(2):
                pool.dma_start(logf_prompt[0, 0, b * P:b * P + P, :], lfr[:, b, :]).then_inc(s_out, 16)
            pool.dma_start(logf_sample[0].rearrange("s t h -> (s t) h"), lfr[0:TS, 2, :]).then_inc(s_out, 16)
            pool.wait_ge(rowT_a, 3)
            pool.wait_ge(rowT_d, 3)
            pool.dma_start(k_prompt[0, 0].rearrange("(b p) h d -> p b (h d)", p=P), k_rows[:, 0:2, :]).then_inc(s_kout, 16)
            pool.dma_start(k_sample[0].rearrange("s t h d -> (s t) (h d)"), k_rows[0:TS, 2, :]).then_inc(s_kout, 16)
            pool.wait_ge(rowT_a, 6)
            pool.wait_ge(rowT_d, 6)
            pool.dma_start(v_prompt[0, 0].rearrange("(b p) h d -> p b (h d)", p=P), v_rows[:, 0:2, :]).then_inc(s_out, 16)
            pool.dma_start(v_sample[0].rearrange("s t h d -> (s t) (h d)"), v_new[0:TS, :]).then_inc(s_out, 16)
            pool.wait_ge(pool_sel, 1)
            pool.wait_ge(cum_done, 1)
            pool.wait_ge(sufT_done, 1)

            def extra_rows(h, j):
                pool.wait_ge(S_max, h + 1)
                for p0, src in ((64, ones), (96, cum_q)):
                    rows = slice(p0, p0 + H)
                    pick = ident[rows, bass.ds(p0 + h, 1)].broadcast_to([H, TP])
                    own.wait()
                    ins = g.tensor_tensor(q_st[j][rows, :], src[rows, 0:TP], pick, ALU.mult)
                    if p0 == 64:
                        own.mark(ins)
                ins.then_inc(qe_ready, 1)
                pool.wait_ge(qe_ready, h + 1)

            def pair_and_sequence(s, j, first):
                extra_rows(2 * s, 0)
                extra_rows(2 * s + 1, 1)
                pool.wait_ge(sS_ps, 2 * s + 1)
                own.mark(g.tensor_copy(cumk_s[:, :], cumk[:, bass.ds(s, 1), :].rearrange("p a n -> p (a n)")))
                own.wait()
                g.tensor_tensor(selq[32:32 + H, :, 0:2 * ST].rearrange("p k (e t) -> p k e t", e=2),
                                sel[32:32 + H, :, :].rearrange("p k (e t) -> p k e t", e=2),
                                cq[32:32 + H, bass.ds(ST * s, ST)].unsqueeze(1).unsqueeze(1).broadcast_to(
                                    [H, KA, 2, ST]), ALU.mult).then_inc(sSel, 1)
                pool.wait_ge(sSel, s + 1)
                if not first:
                    pool.wait_ge(O_ps, 2 * s - 1)
                g.tensor_copy(v_st[j][:, :, :], v_rows[:, 0:2, bass.ds(P * s, P)]).then_inc(v_ready, 1)
                pool.wait_ge(v_ready, s + 1)

            for s in range(2):
                pair_and_sequence(s, s, True)
            with own.loop(PAGE_TURNS - 1, 2 * 3) as i:
                for j in range(2):
                    pair_and_sequence(2 * i + 2 + j, j, False)
            for n, src in ((2, r_T), (4, f_T)):
                pool.wait_ge(rstd_ready, n)
                for c in range(2, 4):
                    v = src[:, SK * c:SK * c + SK, :]
                    g.tensor_tensor(v, v, rstd[:, :].unsqueeze(1).broadcast_to([P, SK, NT]), ALU.mult
                                    ).then_inc(normed, 1)
            for c in range(4):
                pool.wait_ge(y_out, 3 * c + 3)
                cols = slice(SN * c, SN * c + SN)
                pool.dma_start(y_prompt[0].rearrange("(b p) n -> p b n", p=P)[:, :, cols], y_rows[:, 0:2, cols]).then_inc(s_out, 16)
                pool.dma_start(y_sample.rearrange("s t n -> (s t) n")[:, cols], y_rows[0:TS, 2, cols]).then_inc(s_out, 16)
            pool.wait_ge(s_out, 16 * (5 + 8))
            pool.wait_ge(s_kout, 32)
            pool.wait_ge(s_zout, 32)


_INS = ["x_prompt", "x_sample", "cache_k", "cache_v", "cache_logf", "state_conv", "page_table", "c_prompt",
        "c_sample", "w_ada", "b_ada", "g_pre1", "w_in", "b_f", "w_conv", "w_oa", "w_ob", "w_o", "g_post1",
        "g_pre2", "w_ffn_in", "w_ffn_out", "g_post2"]


def kernel(**inputs):
    from concourse import bacc
    from concourse.bass_utils import run_bass_kernel_spmd

    nc = bacc.Bacc("TRN2", target_bir_lowering=False, num_devices=1)
    arrays, args = {}, []
    for name in _INS:
        a = np.ascontiguousarray(inputs[name])
        arrays[f"in_{name}"] = a
        args.append(nc.dram_tensor(f"in_{name}", a.shape, mybir.dt.from_np(a.dtype), kind="ExternalInput").ap())
    B, T, D = arrays["in_x_prompt"].shape
    SB, ST, _ = arrays["in_x_sample"].shape
    L, _, _, H, DH = arrays["in_cache_k"].shape
    _, _, CP, DC = arrays["in_state_conv"].shape
    outs = [(B, T, D), (SB, ST, D), (L, B, T, H, DH), (L, B, T, H, DH), (L, B, T, H), (L, B, CP, DC),
            (L, SB, ST, H, DH), (L, SB, ST, H, DH), (L, SB, ST, H), (L, SB, CP, DC)]
    for i, shape in enumerate(outs):
        args.append(nc.dram_tensor(f"out_{i}", shape, F32, kind="ExternalOutput").ap())
    layer(nc, *args)
    r = run_bass_kernel_spmd(nc, [arrays], core_ids=[0])
    return tuple(r.results[0][f"out_{i}"] for i in range(len(outs)))
```
